# Optimizing a Trainium2 kernel written in Bass

```python
import math
import jax
import jax.numpy as jnp
from jax import lax
import numpy as np

D_MODEL = 1024
BATCH = 1
SEQ = 256
DEPTH = 2

GRID_W = 64
CTX_LEN = 256
N_EVEN = (DEPTH + 1) // 2
N_ODD = DEPTH // 2
N_MOD = 6
FNET_GROUPS = 4
FNET_GROUP_DIM = 128
FNET_WIDTH = FNET_GROUPS * FNET_GROUP_DIM
NA_HEADS = 8
NA_HEAD_DIM = 64
NA_WIDTH = NA_HEADS * NA_HEAD_DIM
NA_KH_MAX = 8
NA_KW = 16
EVEN_IN_WIDTH = FNET_WIDTH + 3 * NA_WIDTH
EVEN_MIX_WIDTH = FNET_WIDTH + NA_WIDTH
GQA_Q_HEADS = 12
GQA_KV_HEADS = 3
GQA_HEAD_DIM = 64
GQA_Q_WIDTH = GQA_Q_HEADS * GQA_HEAD_DIM
GQA_KV_WIDTH = GQA_KV_HEADS * GQA_HEAD_DIM
Q_BLOCK = 128
ROPE_THETA = 10000.0
S5_GROUPS = 16
S5_GROUP_DIM = 16
S5_WIDTH = S5_GROUPS * S5_GROUP_DIM
S5_STATE = 64
S5_DT_MIN = 0.001
S5_DT_MAX = 0.1
ODD_IN_WIDTH = GQA_Q_WIDTH + 2 * GQA_KV_WIDTH + S5_WIDTH
ODD_MIX_WIDTH = GQA_Q_WIDTH + S5_WIDTH
D_FF_DENSE = 2816
N_EXPERTS = 8
TOP_K = 2
D_FF_EXPERT = 3584

EPS = 1e-6
NEG_INF = -1e30

kernel_name = 'hybrid_fourier_natten_gqa_s5_moe_dit'

def rms_norm(x, gain):
    xf = x.astype(jnp.float32)
    y = xf * lax.rsqrt(jnp.mean(xf * xf, axis=-1, keepdims=True) + EPS)
    return (y * gain.astype(jnp.float32)).astype(x.dtype)

def ada_modulation(cond, w_mod, b_mod):
    m = jax.nn.silu(cond) @ w_mod + b_mod
    return jnp.split(m, N_MOD, axis=-1)

def modulate(h, shift, scale):
    return h * (1.0 + scale) + shift

def swiglu(h, w1, w3, w2):
    return (jax.nn.silu(h @ w1) * (h @ w3)) @ w2

def split_heads(t, n_heads, head_dim):
    return t.reshape(t.shape[0], t.shape[1], n_heads, head_dim)

def axial_rope(n_tokens, head_dim):
    t = jnp.arange(n_tokens)
    row = (t // GRID_W).astype(jnp.float32)
    col = (t % GRID_W).astype(jnp.float32)
    n_pairs_axis = head_dim // 4
    freqs = ROPE_THETA ** (-jnp.arange(n_pairs_axis, dtype=jnp.float32) / n_pairs_axis)
    ang = jnp.concatenate([row[:, None] * freqs, col[:, None] * freqs], axis=-1)
    return jnp.cos(ang)[None, :, None, :], jnp.sin(ang)[None, :, None, :]

def apply_rope(x, cos, sin):
    xf = x.astype(jnp.float32)
    x1, x2 = xf[..., 0::2], xf[..., 1::2]
    out = jnp.stack([x1 * cos - x2 * sin, x1 * sin + x2 * cos], axis=-1)
    return out.reshape(x.shape).astype(x.dtype)

def fourier_mix(u):
    b, n, _ = u.shape
    ug = u.astype(jnp.float32).reshape(b, n, FNET_GROUPS, FNET_GROUP_DIM)
    y = jnp.fft.fft2(ug, axes=(1, 3), norm='ortho').real
    return y.reshape(b, n, FNET_WIDTH).astype(u.dtype)

def context_attention(q, k, v):
    b, lq, hq, dh = q.shape
    hkv = k.shape[2]
    qg = q.reshape(b, lq, hkv, hq // hkv, dh)
    s = jnp.einsum('bqhgd,bkhd->bhgqk', qg, k).astype(jnp.float32) * dh ** -0.5
    p = jax.nn.softmax(s, axis=-1).astype(v.dtype)
    o = jnp.einsum('bhgqk,bkhd->bqhgd', p, v)
    return o.reshape(b, lq, hq * dh)

def block_sweep_attention(q, k_all, v_all):
    b, n, hq, dh = q.shape
    hkv = k_all.shape[2]
    g = hq // hkv
    nb = n // Q_BLOCK
    qb = q.reshape(b, nb, Q_BLOCK, hkv, g, dh).transpose(1, 0, 2, 3, 4, 5)

    def one_block(q_blk):
        s = jnp.einsum('bqhgd,bkhd->bhgqk', q_blk, k_all).astype(jnp.float32) * dh ** -0.5
        p = jax.nn.softmax(s, axis=-1).astype(v_all.dtype)
        return jnp.einsum('bhgqk,bkhd->bqhgd', p, v_all)

    o = lax.map(one_block, qb)
    return o.transpose(1, 0, 2, 3, 4, 5).reshape(b, n, hq * dh)

def neighbourhood_attention(q, k, v, k_ctx, v_ctx, rpb):
    b, n, h, dh = q.shape
    rows = n // GRID_W
    kh = min(NA_KH_MAX, rows)
    qg = q.reshape(b, rows, GRID_W, h, dh)
    kg = k.reshape(b, rows, GRID_W, h, dh)
    vg = v.reshape(b, rows, GRID_W, h, dh)
    qcol = jnp.arange(GRID_W)
    kcol = jnp.arange(GRID_W)
    col_start = jnp.clip(qcol - NA_KW // 2, 0, GRID_W - NA_KW)
    col_in = (kcol[None, :] >= col_start[:, None]) & (kcol[None, :] < col_start[:, None] + NA_KW)
    mask = jnp.broadcast_to(col_in[:, None, :], (GRID_W, kh, GRID_W)).reshape(GRID_W, kh * GRID_W)
    dc_idx = jnp.clip(kcol[None, :] - qcol[:, None] + NA_KW - 1, 0, 2 * NA_KW - 2)
    scale = dh ** -0.5

    def one_row(r):
        r0 = jnp.clip(r - kh // 2, 0, rows - kh)
        kb = lax.dynamic_slice_in_dim(kg, r0, kh, axis=1).reshape(b, kh * GRID_W, h, dh)
        vb = lax.dynamic_slice_in_dim(vg, r0, kh, axis=1).reshape(b, kh * GRID_W, h, dh)
        qr = lax.dynamic_index_in_dim(qg, r, axis=1, keepdims=False)
        dr_idx = r0 + jnp.arange(kh) - r + NA_KH_MAX - 1
        bias = rpb[:, dr_idx][:, :, dc_idx]
        bias = bias.transpose(0, 2, 1, 3).reshape(h, GRID_W, kh * GRID_W).astype(jnp.float32)
        s_loc = jnp.einsum('bqhd,bkhd->bhqk', qr, kb).astype(jnp.float32) * scale + bias
        s_loc = jnp.where(mask, s_loc, NEG_INF)
        s_ctx = jnp.einsum('bqhd,bkhd->bhqk', qr, k_ctx).astype(jnp.float32) * scale
        p = jax.nn.softmax(jnp.concatenate([s_loc, s_ctx], axis=-1), axis=-1).astype(v.dtype)
        n_loc = kh * GRID_W
        return (jnp.einsum('bhqk,bkhd->bqhd', p[..., :n_loc], vb)
                + jnp.einsum('bhqk,bkhd->bqhd', p[..., n_loc:], v_ctx))

    o = lax.map(one_row, jnp.arange(rows))
    return o.transpose(1, 0, 2, 3, 4).reshape(b, n, h * dh)

def _linear_combine(left, right):
    a_l, b_l = left
    a_r, b_r = right
    return a_r * a_l, a_r * b_l + b_r

def linear_recurrence(lam_bar, bu, s0):
    if s0 is not None:
        bu = bu.at[:, 0].add(lam_bar * s0)
    a = jnp.broadcast_to(lam_bar, bu.shape)
    _, states = lax.associative_scan(_linear_combine, (a, bu), axis=1)
    return states

def s5_direction(ug_lat, ug_ctx, a_re, a_im, log_step, b_re, b_im, c_re, c_im, reverse, with_ctx_out):
    lam = lax.complex(a_re.astype(jnp.float32), a_im.astype(jnp.float32))
    step = jnp.exp(log_step.astype(jnp.float32))[:, None]
    lam_bar = jnp.exp(lam * step)
    b_mat = lax.complex(b_re.astype(jnp.float32), b_im.astype(jnp.float32))
    b_bar = ((lam_bar - 1.0) / lam)[..., None] * b_mat
    c_mat = lax.complex(c_re.astype(jnp.float32), c_im.astype(jnp.float32))

    def orient(z):
        return jnp.flip(z, axis=1) if reverse else z

    bu_ctx = jnp.einsum('blgn,gpn->blgp', orient(ug_ctx).astype(jnp.complex64), b_bar)
    st_ctx = linear_recurrence(lam_bar, bu_ctx, None)
    bu_lat = jnp.einsum('blgn,gpn->blgp', orient(ug_lat).astype(jnp.complex64), b_bar)
    st_lat = linear_recurrence(lam_bar, bu_lat, st_ctx[:, -1])
    y_lat = orient(jnp.einsum('blgp,gnp->blgn', st_lat, c_mat).real)
    y_ctx = orient(jnp.einsum('blgp,gnp->blgn', st_ctx, c_mat).real) if with_ctx_out else None
    return y_lat, y_ctx

def s5_mixer(u_lat, u_ctx, a_re, a_im, log_step, b_re, b_im, c_re, c_im, d_skip, glu_w, glu_b, with_ctx_out):
    def groups(u):
        return u.astype(jnp.float32).reshape(u.shape[0], u.shape[1], S5_GROUPS, S5_GROUP_DIM)

    ug_lat, ug_ctx = groups(u_lat), groups(u_ctx)
    y_lat, y_ctx = None, None
    for direction, reverse in ((0, False), (1, True)):
        yl, yc = s5_direction(ug_lat, ug_ctx, a_re[direction], a_im[direction], log_step[direction],
                              b_re[direction], b_im[direction], c_re[direction], c_im[direction],
                              reverse, with_ctx_out)
        y_lat = yl if y_lat is None else y_lat + yl
        if with_ctx_out:
            y_ctx = yc if y_ctx is None else y_ctx + yc

    def readout(u, y):
        y = y.reshape(u.shape) + d_skip.astype(jnp.float32) * u.astype(jnp.float32)
        y = jax.nn.gelu(y).astype(u.dtype)
        return y * jax.nn.sigmoid(y @ glu_w + glu_b)

    out_ctx = readout(u_ctx, y_ctx) if with_ctx_out else None
    return readout(u_lat, y_lat), out_ctx

def moe_swiglu(h, router_w, router_b, w1, w3, w2):
    shape = h.shape
    t = h.reshape(-1, shape[-1])
    logits = (t @ router_w + router_b).astype(jnp.float32)
    top_val, top_idx = lax.top_k(logits, TOP_K)
    top_w = jax.nn.softmax(top_val, axis=-1)
    gates = jnp.einsum('tk,tke->te', top_w,
                       jax.nn.one_hot(top_idx, N_EXPERTS, dtype=jnp.float32)).astype(t.dtype)
    out = jnp.zeros_like(t)
    for e in range(N_EXPERTS):
        out = out + gates[:, e:e + 1] * swiglu(t, w1[e], w3[e], w2[e])
    return out.reshape(shape)

def even_layer(x, xc, c, c_ctx, mod_w, mod_b, norm_mix, norm_ffn, w_in, q_gain, k_gain, rpb, w_out,
               w1, w3, w2, update_ctx):
    sh1, sc1, g1, sh2, sc2, g2 = ada_modulation(c[:, None, :], mod_w, mod_b)
    csh1, csc1, cg1, csh2, csc2, cg2 = ada_modulation(c_ctx, mod_w, mod_b)
    cuts = [FNET_WIDTH, FNET_WIDTH + NA_WIDTH, FNET_WIDTH + 2 * NA_WIDTH]
    h = modulate(rms_norm(x, norm_mix), sh1, sc1) @ w_in
    hc = modulate(rms_norm(xc, norm_mix), csh1, csc1) @ w_in
    u, q, k, v = jnp.split(h, cuts, axis=-1)
    uc, qc, kc, vc = jnp.split(hc, cuts, axis=-1)
    q = rms_norm(split_heads(q, NA_HEADS, NA_HEAD_DIM), q_gain)
    k = rms_norm(split_heads(k, NA_HEADS, NA_HEAD_DIM), k_gain)
    v = split_heads(v, NA_HEADS, NA_HEAD_DIM)
    kc = rms_norm(split_heads(kc, NA_HEADS, NA_HEAD_DIM), k_gain)
    vc = split_heads(vc, NA_HEADS, NA_HEAD_DIM)
    o_lat = jnp.concatenate([fourier_mix(u), neighbourhood_attention(q, k, v, kc, vc, rpb)], axis=-1)
    x = x + g1 * (o_lat @ w_out)
    if update_ctx:
        qc = rms_norm(split_heads(qc, NA_HEADS, NA_HEAD_DIM), q_gain)
        o_ctx = jnp.concatenate([fourier_mix(uc), context_attention(qc, kc, vc)], axis=-1)
        xc = xc + cg1 * (o_ctx @ w_out)
    x = x + g2 * swiglu(modulate(rms_norm(x, norm_ffn), sh2, sc2), w1, w3, w2)
    if update_ctx:
        xc = xc + cg2 * swiglu(modulate(rms_norm(xc, norm_ffn), csh2, csc2), w1, w3, w2)
    return x, xc

def odd_layer(x, xc, c, c_ctx, mod_w, mod_b, norm_mix, norm_ffn, w_in, q_gain, k_gain,
              a_re, a_im, log_step, b_re, b_im, c_re, c_im, d_skip, glu_w, glu_b, w_out,
              router_w, router_b, ew1, ew3, ew2, update_ctx):
    sh1, sc1, g1, sh2, sc2, g2 = ada_modulation(c[:, None, :], mod_w, mod_b)
    csh1, csc1, cg1, csh2, csc2, cg2 = ada_modulation(c_ctx, mod_w, mod_b)
    cuts = [GQA_Q_WIDTH, GQA_Q_WIDTH + GQA_KV_WIDTH, GQA_Q_WIDTH + 2 * GQA_KV_WIDTH]
    h = modulate(rms_norm(x, norm_mix), sh1, sc1) @ w_in
    hc = modulate(rms_norm(xc, norm_mix), csh1, csc1) @ w_in
    q, k, v, u = jnp.split(h, cuts, axis=-1)
    qc, kc, vc, uc = jnp.split(hc, cuts, axis=-1)
    cos, sin = axial_rope(x.shape[1], GQA_HEAD_DIM)
    q = apply_rope(rms_norm(split_heads(q, GQA_Q_HEADS, GQA_HEAD_DIM), q_gain), cos, sin)
    k = apply_rope(rms_norm(split_heads(k, GQA_KV_HEADS, GQA_HEAD_DIM), k_gain), cos, sin)
    v = split_heads(v, GQA_KV_HEADS, GQA_HEAD_DIM)
    kc = rms_norm(split_heads(kc, GQA_KV_HEADS, GQA_HEAD_DIM), k_gain)
    vc = split_heads(vc, GQA_KV_HEADS, GQA_HEAD_DIM)
    k_all = jnp.concatenate([kc, k], axis=1)
    v_all = jnp.concatenate([vc, v], axis=1)
    o_attn = block_sweep_attention(q, k_all, v_all)
    o_ssm, oc_ssm = s5_mixer(u, uc, a_re, a_im, log_step, b_re, b_im, c_re, c_im, d_skip, glu_w, glu_b,
                             update_ctx)
    x = x + g1 * (jnp.concatenate([o_attn, o_ssm], axis=-1) @ w_out)
    if update_ctx:
        qc = rms_norm(split_heads(qc, GQA_Q_HEADS, GQA_HEAD_DIM), q_gain)
        o_ctx = jnp.concatenate([context_attention(qc, kc, vc), oc_ssm], axis=-1)
        xc = xc + cg1 * (o_ctx @ w_out)
    x = x + g2 * moe_swiglu(modulate(rms_norm(x, norm_ffn), sh2, sc2), router_w, router_b, ew1, ew3, ew2)
    if update_ctx:
        xc = xc + cg2 * moe_swiglu(modulate(rms_norm(xc, norm_ffn), csh2, csc2),
                                   router_w, router_b, ew1, ew3, ew2)
    return x, xc

def setup_inputs(seed: int = 0) -> dict:
    key = jax.random.key(seed)
    keys = iter(jax.random.split(key, 64))

    def normal(shape, scale):
        return scale * jax.random.normal(next(keys), shape, jnp.float32)

    def gain(shape):
        return 1.0 + normal(shape, 0.05)

    d = D_MODEL
    ne, no = N_EVEN, N_ODD
    s5_shape = (no, 2, S5_GROUPS, S5_STATE)
    n_idx = jnp.arange(S5_STATE, dtype=jnp.float32)
    log_lo, log_hi = math.log(S5_DT_MIN), math.log(S5_DT_MAX)
    inp = {}
    inp['x'] = normal((BATCH, SEQ, d), 1.0)
    inp['c'] = normal((BATCH, d), 1.0)
    inp['ctx'] = normal((BATCH, CTX_LEN, d), 1.0)
    inp['c_ctx'] = normal((d,), 0.5)
    inp['ev_mod_w'] = normal((ne, d, N_MOD * d), 0.5 * d ** -0.5)
    inp['ev_mod_b'] = normal((ne, N_MOD * d), 0.02)
    inp['ev_norm_mix'] = gain((ne, d))
    inp['ev_norm_ffn'] = gain((ne, d))
    inp['ev_w_in'] = normal((ne, d, EVEN_IN_WIDTH), d ** -0.5)
    inp['ev_q_gain'] = gain((ne, NA_HEAD_DIM))
    inp['ev_k_gain'] = gain((ne, NA_HEAD_DIM))
    inp['ev_rpb'] = normal((ne, NA_HEADS, 2 * NA_KH_MAX - 1, 2 * NA_KW - 1), 0.1)
    inp['ev_w_out'] = normal((ne, EVEN_MIX_WIDTH, d), EVEN_MIX_WIDTH ** -0.5)
    inp['ev_ffn_w1'] = normal((ne, d, D_FF_DENSE), d ** -0.5)
    inp['ev_ffn_w3'] = normal((ne, d, D_FF_DENSE), d ** -0.5)
    inp['ev_ffn_w2'] = normal((ne, D_FF_DENSE, d), D_FF_DENSE ** -0.5)
    inp['od_mod_w'] = normal((no, d, N_MOD * d), 0.5 * d ** -0.5)
    inp['od_mod_b'] = normal((no, N_MOD * d), 0.02)
    inp['od_norm_mix'] = gain((no, d))
    inp['od_norm_ffn'] = gain((no, d))
    inp['od_w_in'] = normal((no, d, ODD_IN_WIDTH), d ** -0.5)
    inp['od_q_gain'] = gain((no, GQA_HEAD_DIM))
    inp['od_k_gain'] = gain((no, GQA_HEAD_DIM))
    inp['od_s5_a_re'] = -0.5 + normal(s5_shape, 0.01)
    inp['od_s5_a_im'] = jnp.pi * n_idx + normal(s5_shape, 0.01)
    inp['od_s5_log_step'] = log_lo + (log_hi - log_lo) * jax.random.uniform(
        next(keys), (no, 2, S5_GROUPS), jnp.float32)
    inp['od_s5_b_re'] = normal((no, 2, S5_GROUPS, S5_STATE, S5_GROUP_DIM), S5_GROUP_DIM ** -0.5)
    inp['od_s5_b_im'] = normal((no, 2, S5_GROUPS, S5_STATE, S5_GROUP_DIM), S5_GROUP_DIM ** -0.5)
    inp['od_s5_c_re'] = normal((no, 2, S5_GROUPS, S5_GROUP_DIM, S5_STATE), S5_STATE ** -0.5)
    inp['od_s5_c_im'] = normal((no, 2, S5_GROUPS, S5_GROUP_DIM, S5_STATE), S5_STATE ** -0.5)
    inp['od_s5_d'] = normal((no, S5_WIDTH), 1.0)
    inp['od_s5_glu_w'] = normal((no, S5_WIDTH, S5_WIDTH), S5_WIDTH ** -0.5)
    inp['od_s5_glu_b'] = normal((no, S5_WIDTH), 0.02)
    inp['od_w_out'] = normal((no, ODD_MIX_WIDTH, d), ODD_MIX_WIDTH ** -0.5)
    inp['od_router_w'] = normal((no, d, N_EXPERTS), d ** -0.5)
    inp['od_router_b'] = normal((no, N_EXPERTS), 0.01)
    inp['od_exp_w1'] = normal((no, N_EXPERTS, d, D_FF_EXPERT), d ** -0.5)
    inp['od_exp_w3'] = normal((no, N_EXPERTS, d, D_FF_EXPERT), d ** -0.5)
    inp['od_exp_w2'] = normal((no, N_EXPERTS, D_FF_EXPERT, d), D_FF_EXPERT ** -0.5)
    return inp

def reference(x, c, ctx, c_ctx,
              ev_mod_w, ev_mod_b, ev_norm_mix, ev_norm_ffn, ev_w_in, ev_q_gain, ev_k_gain, ev_rpb, ev_w_out,
              ev_ffn_w1, ev_ffn_w3, ev_ffn_w2,
              od_mod_w, od_mod_b, od_norm_mix, od_norm_ffn, od_w_in, od_q_gain, od_k_gain,
              od_s5_a_re, od_s5_a_im, od_s5_log_step, od_s5_b_re, od_s5_b_im, od_s5_c_re, od_s5_c_im,
              od_s5_d, od_s5_glu_w, od_s5_glu_b, od_w_out,
              od_router_w, od_router_b, od_exp_w1, od_exp_w3, od_exp_w2):
    xc = ctx
    for layer in range(DEPTH):
        update_ctx = layer < DEPTH - 1
        j = layer // 2
        if layer % 2 == 0:
            x, xc = even_layer(x, xc, c, c_ctx, ev_mod_w[j], ev_mod_b[j], ev_norm_mix[j], ev_norm_ffn[j],
                               ev_w_in[j], ev_q_gain[j], ev_k_gain[j], ev_rpb[j], ev_w_out[j],
                               ev_ffn_w1[j], ev_ffn_w3[j], ev_ffn_w2[j], update_ctx)
        else:
            x, xc = odd_layer(x, xc, c, c_ctx, od_mod_w[j], od_mod_b[j], od_norm_mix[j], od_norm_ffn[j],
                              od_w_in[j], od_q_gain[j], od_k_gain[j],
                              od_s5_a_re[j], od_s5_a_im[j], od_s5_log_step[j], od_s5_b_re[j], od_s5_b_im[j],
                              od_s5_c_re[j], od_s5_c_im[j], od_s5_d[j], od_s5_glu_w[j], od_s5_glu_b[j],
                              od_w_out[j], od_router_w[j], od_router_b[j],
                              od_exp_w1[j], od_exp_w3[j], od_exp_w2[j], update_ctx)
    return x


_drawn_inputs = setup_inputs


def setup_inputs(seed=0):
    import zlib

    import numpy as np

    out = dict(_drawn_inputs(seed))
    spreads = {}
    factors = {'ev_norm_mix': 5.166,
     'ev_norm_ffn': 2.826,
     'ev_q_gain': 7.717,
     'ev_k_gain': 7.757,
     'ev_rpb': 8.0,
     'od_mod_b': 3.049,
     'od_norm_mix': 7.168,
     'od_q_gain': 8.0,
     'od_k_gain': 8.0,
     'od_s5_a_re': 64.0,
     'od_s5_a_im': 18.121,
     'od_s5_log_step': 16.479,
     'od_s5_b_re': 26.412,
     'od_s5_b_im': 29.067,
     'od_s5_c_re': 30.035,
     'od_s5_c_im': 33.296,
     'od_s5_glu_b': 64.0,
     'od_router_b': 63.357,
     'od_norm_ffn': 6.871}
    for name, (base, spread) in spreads.items():
        noise = np.random.default_rng([zlib.crc32(name.encode()), seed]).standard_normal(out[name].shape)
        drawn = base * np.exp(spread * noise) if base else spread * noise
        out[name] = jnp.asarray(drawn.astype(out[name].dtype))
    for name, factor in factors.items():
        out[name] = (out[name] * factor).astype(out[name].dtype)
    return out
```

```python
from contextlib import ExitStack

import numpy as np

import concourse.bass as bass
from concourse import mybir

F32 = mybir.dt.float32
I32 = mybir.dt.int32
ALU = mybir.AluOpType
ACT = mybir.ActivationFunctionType
AX = mybir.AxisListType.X

P = 128
D = 1024
DC = D // P
SEQ = CTX = 256
GRID_W = 64
LAT_TILES, TILES = SEQ // P, (SEQ + CTX) // P
TOK = SEQ + CTX
HD = 64
NA_HEADS, NA_KW, NA_DR = 8, 16, 15
ROWS = SEQ // GRID_W
QH, KVH = 12, 3
S5_GROUPS, S5_DIM, S5_STATE = 16, 16, 64
PAIRS = S5_GROUPS // 2
UNITS = 2 * PAIRS
FF = 2816
FC = FF // P
NE, FE = 8, 3584
EC = FE // P
EPS = 1e-6
RPB_PAD = 127

RING, SLOT = 6, 4096
S_MOD = [0, 35]
S_IN_E, S_OUT_E, S_UP, S_DOWN = 12, 16, 18, 29
S_IN_O, S_OUT_O, S_MOE = 47, 51, 53
UP_SLOTS, DOWN_SLOTS = FC // 2, [8, 8, 6]
W13_SLOTS, W2_SLOTS = EC // 2, EC // 4
E_SLOTS = W13_SLOTS + W2_SLOTS

C_ID, C_REV, C_TRI, C_ONE, C_IOTA, C_MASK, C_COS, C_SIN = 0, 128, 256, 384, 512, 640, 704, 832
C_ALL = 960
V_COND, V_NORM, V_MODB, V_ARE, V_AIM, V_STEP, V_D, V_GLUB = 0, 16, 48, 144, 160, 176, 192, 194
V_HEAD, V_RB = 196, 452
V_RW = 460
V_ALL = 524
H_EQ, H_EK, H_OQ, H_OK = range(4)
M_SH1, M_SC1, M_G1, M_SH2, M_SC2, M_G2 = range(0, 48, 8)


S_R, S_PW = 21, 22
ROUND = 12582912.0
LN2_PARTS = (0.693359375, float(np.log(2) - 0.693359375))
TURN_PARTS = (6.28125, 0.0019340515136718750, float(2 * np.pi - 6.28125 - 0.0019340515136718750))


def constants():
    c = np.zeros((P, C_ALL), np.float32)
    i = np.arange(P)
    c[i, C_ID + i] = 1.0
    c[i, C_REV + P - 1 - i] = 1.0
    c[:, C_TRI:C_TRI + P] = i[:, None] < i[None, :]
    c[:, C_ONE:C_ONE + P] = 1.0
    c[:, C_IOTA:C_IOTA + P] = i[None, :]
    q, k = (i % GRID_W)[:, None], np.arange(GRID_W)[None, :]
    start = np.clip(q - NA_KW // 2, 0, GRID_W - NA_KW)
    c[:, C_MASK:C_MASK + GRID_W] = np.where((k >= start) & (k < start + NA_KW), 0.0, -1e30)
    freq = 10000.0 ** (-np.arange(HD // 4, dtype=np.float32) / np.float32(HD // 4))
    for t in range(LAT_TILES):
        tok = t * P + i
        ang = np.concatenate([(tok // GRID_W)[:, None].astype(np.float32) * freq,
                              (tok % GRID_W)[:, None].astype(np.float32) * freq], 1).astype(np.float32)
        cos, sin = np.cos(ang), np.sin(ang)
        c[:, C_COS + t * HD:C_COS + (t + 1) * HD] = np.repeat(cos, 2, 1)
        c[:, C_SIN + t * HD:C_SIN + (t + 1) * HD] = np.stack([-sin, sin], 2).reshape(P, HD)
    return c


def dft_constants():
    n = np.arange(SEQ)
    ang = 2 * np.pi * ((n[:, None] * n[None, :]) % SEQ) / SEQ
    tok = np.concatenate([np.cos(ang), np.sin(ang)], 1).reshape(2, P, 2 * SEQ).transpose(1, 0, 2)
    n = np.arange(P)
    ang = 2 * np.pi * ((n[:, None] * n[None, :]) % P) / P
    ch = np.concatenate([np.cos(ang), -np.sin(ang)], 1) / np.sqrt(SEQ * P)
    return np.concatenate([tok.reshape(P, 4 * SEQ), ch], 1).astype(np.float32)


def build(nc, a, out, stop=99):
    ctx = ExitStack()
    with ctx:
        def sb(name, shape, dt=F32):
            return ctx.enter_context(nc.sbuf_tensor(name, shape, dt))

        def sem(name):
            return ctx.enter_context(nc.semaphore(name))

        bank = [ctx.enter_context(nc.psum_tensor(f"bank{i}", [P, 512], F32)) for i in range(8)]
        ring = sb("ring", [P, RING, SLOT])
        X = sb("X", [P, TILES, D])
        HT = sb("HT", [P, 4096])
        B = sb("B", [P, FC * TOK])
        S = sb("S", [P, 6656])
        cst = sb("cst", [P, C_ALL])
        vec = sb("vec", [P, V_ALL])
        silc = sb("silc", [P, DC, 2])
        mod = [sb(f"mod{i}", [P, 48, 2]) for i in range(2)]
        coef = sb("coef", [P, 4, DC, 2])
        ss = sb("ss", [P, TILES])
        rstd = sb("rstd", [P, TILES])
        hss = sb("hss", [P, QH])
        nmax = sb("nmax", [P, 4])
        rsum = sb("rsum", [P, 4])
        rinv = sb("rinv", [P, 4])

        ident = cst[:, C_ID:C_ID + P]
        rev = cst[:, C_REV:C_REV + P]
        hT = HT[:, :].rearrange("p (c t) -> p c t", c=DC)
        xn = B[:, 0:TILES * D].rearrange("p (t d) -> p t d", t=TILES)
        gT = B[:, :].rearrange("p (c t) -> p c t", c=FC)
        hn = B[:, 0:4 * TOK * 4].rearrange("p (n t c) -> p n t c", n=4, t=TILES)
        oT = B[:, 2048:2048 + DC * TOK].rearrange("p (c t) -> p c t", c=DC)
        G = S[:, 0:2 * D].rearrange("p (s d) -> p s d", s=2)
        mrow = S[:, 4096:5120].rearrange("p (b n) -> p b n", b=2)
        sq = S[:, 2048:3072].rearrange("p (b n) -> p b n", b=2)
        tmp = S[:, 2048:3072].rearrange("p (b n) -> p b n", b=2)
        sil = S[:, 3072:4096].rearrange("p (b n) -> p b n", b=2)
        T1 = S[:, 4096:5120].rearrange("p (b n) -> p b n", b=2)
        dft = S[:, 5120:6400]
        bias = S[:, 0:1024].rearrange("p (b n) -> p b n", b=2)
        bias_raw = B[:, 8192:9216].rearrange("p (b n) -> p b n", b=2)
        prob = S[:, 1024:2560].rearrange("p (b n) -> p b n", b=3)
        pT = S[:, 2560:4608].rearrange("p (b k q) -> p b k q", b=2, k=4)

        s5v = sb("s5v", [P, 32, UNITS])
        flag = sb("flag", [P, 1], I32)
        qn = B[:, 0:1536].rearrange("p (t c) -> p t c", t=2)
        kn = B[:, 1536:3072].rearrange("p (t h b d) -> p t h b d", t=TILES, h=KVH, b=2)
        vn = B[:, 3072:3840].rearrange("p (t c) -> p t c", t=TILES)
        un = B[:, 3840:4864].rearrange("p (t c) -> p t c", t=TILES)
        oTo = B[:, 4864:6912].rearrange("p (c t) -> p c t", c=DC)
        uT = [B[:, 6912 + 1024 * d:7936 + 1024 * d].rearrange("p (c t) -> p c t", c=2) for d in range(2)]
        BT = [B[:, 8960 + 512 * i:9472 + 512 * i] for i in range(2)]
        C5 = [B[:, 9984 + 512 * i:10496 + 512 * i].rearrange("p (u n) -> p u n", u=UNITS) for i in range(2)]
        gluw = B[:, 1536:2048].rearrange("p (k n) -> p k n", k=2)
        qTo = HT[:, 0:1536].rearrange("p (c t) -> p c t", c=6)
        kTo = HT[:, 1536:3072].rearrange("p (c t) -> p c t", c=KVH)
        s_out = HT[:, 3072:4096].rearrange("p (b i t) -> p b i t", b=2, i=2)
        rope_t = S[:, 3072:3584]
        b_raw = [S[:, 5120 + 512 * i:5632 + 512 * i].rearrange("p (u n) -> p u n", u=UNITS) for i in range(2)]
        b_bar = [S[:, 512 * i:512 * i + 512].rearrange("p (u n) -> p u n", u=UNITS) for i in range(2)]
        lo = [S[:, 256 * i:256 * i + 256].rearrange("p (u n) -> p u n", u=UNITS) for i in range(2)]
        hi = [S[:, 512 + 512 * i:1024 + 512 * i].rearrange("p (u n) -> p u n", u=UNITS) for i in range(2)]
        turn = S[:, 1536:3584].rearrange("p (b i t) -> p b i t", b=2, i=2)
        pt = [S[:, 3584 + 512 * i:4096 + 512 * i] for i in range(2)]
        z = [S[:, 4608 + 512 * i:5120 + 512 * i] for i in range(2)]
        vt = [S[:, 5632 + 512 * i:6144 + 512 * i] for i in range(2)]
        b_tmp = S[:, 3584:4096].rearrange("p (u n) -> p u n", u=UNITS)
        p4 = [S[:, 1536 + 256 * i:1792 + 256 * i] for i in range(4)]
        y5 = S[:, 5632:6144].rearrange("p (c t) -> p c t", c=2)
        y5s = S[:, 6144:6656].rearrange("p (c t) -> p c t", c=2)

        pick = B[:, 2048:4352].rearrange("p (t e s) -> p t e s", t=2, e=NE + 1)
        gTall = B[:, 4352:6400].rearrange("p (e t) -> p e t", e=NE)
        acc = B[:, 6400:8448].rearrange("p (t d) -> p t d", t=2)
        gpick = B[:, 8448:10496].rearrange("p (t e s) -> p t e s", t=2, e=NE)
        xe = HT[:, 0:2048].rearrange("p (b c s) -> p b c s", b=2, c=DC)
        ye = HT[:, 2048:3072]
        gTe = HT[:, 3072:3584].rearrange("p (b t) -> p b t", b=2)
        heT = S[:, 0:EC * P].rearrange("p (c s) -> p c s", c=EC)
        he = S[:, 3584:4096].rearrange("p (b n) -> p b n", b=2)
        sile = S[:, 4096:4608].rearrange("p (b n) -> p b n", b=2)
        G2 = S[:, 5120:6144]

        slot_landed = [sem(f"slot{i}_landed") for i in range(RING)]
        vec_landed, cst_landed, x_landed, dft_landed = (
            sem("vec_landed"), sem("cst_landed"), sem("x_landed"), sem("dft_landed"))
        dve_step, act_step, pool_step = sem("dve_step"), sem("act_step"), sem("pool_step")
        cond_ready, mod_psum, mod_row, mod_turned, mod_ready = (
            sem("cond_ready"), sem("mod_psum"), sem("mod_row"), sem("mod_turned"), sem("mod_ready"))
        coef_ready, square_sum, xn_ready, xn_turned, ht_act, ht_dve = (
            sem("coef_ready"), sem("square_sum"), sem("xn_ready"), sem("xn_turned"), sem("ht_act"), sem("ht_dve"))
        in_psum, in_copied, in_squared, in_summed, in_normed, head_ready = (
            sem("in_psum"), sem("in_copied"), sem("in_squared"), sem("in_summed"), sem("in_normed"), sem("head_ready"))
        qk_turned, qk_act, qk_dve = sem("qk_turned"), sem("qk_act"), sem("qk_dve")
        four_a, four_t, four_b, four_o = sem("four_a"), sem("four_t"), sem("four_b"), sem("four_o")
        bias_landed = [sem("bias0_landed"), sem("bias1_landed")]
        bias_ready, bias_used = sem("bias_ready"), sem("bias_used")
        scores, row_max, exp_done, prob_ready, prob_turned, pt_ready, o_psum, o_ready = (
            sem("scores"), sem("row_max"), sem("exp_done"), sem("prob_ready"), sem("prob_turned"),
            sem("pt_ready"), sem("o_psum"), sem("o_ready"))
        gate_psum, gate_ready = sem("gate_psum"), sem("gate_ready")
        res_psum, res_gated, res_done = sem("res_psum"), sem("res_gated"), sem("res_done")
        up_psum, up_silu, up_gated = sem("up_psum"), sem("up_silu"), sem("up_gated")
        mean_ready, root_ready = sem("mean_ready"), sem("root_ready")
        down_read = sem("down_read")
        s5_rden, s5_raw, s5_c, s5_bbar, s5_turned, s5_bt_act, s5_bt_dve = (
            sem("s5_rden"), sem("s5_raw"), sem("s5_c"), sem("s5_bbar"), sem("s5_turned"),
            sem("s5_bt_act"), sem("s5_bt_dve"))
        s5_small, s5_table, s5_bu, s5_bu_used, s5_s, s5_y = (
            sem("s5_small"), sem("s5_table"), sem("s5_bu"), sem("s5_bu_used"), sem("s5_s"), sem("s5_y"))
        y5_ready, y5_gelu, glu_landed, glu_psum, glu_sig, ssm_ready = (
            sem("y5_ready"), sem("y5_gelu"), sem("glu_landed"), sem("glu_psum"), sem("glu_sig"), sem("ssm_ready"))
        logits, top_gap, top_exp, sel_ready, ranks, flag_ready = (
            sem("logits"), sem("top_gap"), sem("top_exp"), sem("sel_ready"), sem("ranks"), sem("flag_ready"))
        pick_ready, gpick_turned, gta_act, gta_dve = (
            sem("pick_ready"), sem("gpick_turned"), sem("gta_act"), sem("gta_dve"))
        e_gather, xe_act, xe_dve, e_up, e_silu, e_gated, e_turned, e_heT = (
            sem("e_gather"), sem("xe_act"), sem("xe_dve"), sem("e_up"), sem("e_silu"), sem("e_gated"),
            sem("e_turned"), sem("e_heT"))
        e_down, y_act, y_dve, e_scatter, e_added, gte_ready = (
            sem("e_down"), sem("y_act"), sem("y_dve"), sem("e_scatter"), sem("e_added"), sem("gte_ready"))
        final_ready, slots_reused = sem("final_ready"), sem("slots_reused")
        out_done = sem("out_done")

        block = ctx.enter_context(nc.Block())

        def slot(i):
            return ring[:, i % RING, :]

        def wait_slot(eng, i):
            eng.wait_ge(slot_landed[i % RING], 32 * (i // RING + 1))

        def read(i):
            if i < S_IN_E:
                return mod_psum, i + 1
            if i < S_OUT_E:
                return in_psum, 4 * (i - S_IN_E + 1)
            if i < S_UP:
                return res_psum, 4 * (i - S_OUT_E + 1)
            if i < S_DOWN:
                return up_psum, 2 * (i - S_UP + 1)
            if i < S_MOD[1]:
                half, j = divmod(i - S_DOWN, 3)
                return (down_read, 2 * half + j + 1) if j < 2 else (res_psum, 12 + 4 * half)
            if i < S_IN_O:
                return mod_psum, 12 + i - S_MOD[1] + 1
            if i < S_OUT_O:
                return in_psum, 16 + [2, 4, 8, 12][i - S_IN_O]
            return res_psum, 16 + 2 * (i - S_OUT_O + 1)

        IN_COLS = [(0, 512), (512, 256), (768, 384), (1152, 256)]
        IN_JOBS = [(n, t) for n in range(4) for t in range(LAT_TILES if n < 2 else TILES)]
        ATTN_E = 4 * NA_HEADS

        NORMS = [(0, M_SH1, M_SC1, 4, 0), (0, M_SH2, M_SC2, 4, 8),
                 (1, M_SH1, M_SC1, 4, 16), (1, M_SH2, M_SC2, 2, 20)]
        GATES = [(0, M_G1, 2), (0, M_G2, 2), (1, M_G1, 1), (1, M_G2, 1)]

        qT, kT = hT[:, 0:4], hT[:, 4:8]

        def even_jobs():
            jobs = []
            for h in range(NA_HEADS):
                rows = slice(64 * (h % 2), 64 * (h % 2) + HD)
                for t in range(2):
                    jobs.append((qT[rows, h // 2, t * P:(t + 1) * P], kT[rows, h // 2, :], TOK,
                                 [hn[:, 3, k, h * HD:(h + 1) * HD] for k in range(4)], h % 2, h, 0))
            for h in range(NA_HEADS):
                rows = slice(64 * (h % 2), 64 * (h % 2) + HD)
                for t in range(2, 4):
                    jobs.append((qT[rows, h // 2, t * P:(t + 1) * P], kT[rows, h // 2, SEQ:], CTX,
                                 [hn[:, 3, 2 + k, h * HD:(h + 1) * HD] for k in range(2)], h % 2, h, 1))
            return jobs

        EVEN_JOBS = even_jobs()
        ODD_JOBS = [(qTo[64 * (h % 2):64 * (h % 2) + HD, h // 2, t * P:(t + 1) * P],
                     kTo[64 * (h % 2):64 * (h % 2) + HD, h // 4, :], TOK,
                     [vn[:, k, (h // 4) * HD:(h // 4 + 1) * HD] for k in range(4)], h % 2, h, 0)
                    for h in range(QH) for t in range(2)]
        (R_L, R_EQ, R_L2, R_C, R_O1, R_O2, R_SEL, R_GATE, R_POS, R_POS2, R_T) = range(11)

        @block.sync
        def _(sp):
            def load(i, halves):
                if i >= RING:
                    sp.wait_ge(*read(i - RING))
                for dst, src in halves:
                    sp.dma_start(dst, src).then_inc(slot_landed[i % RING], 16)

            def columns(i, w, lo, n, chunks=range(DC)):
                k = len(chunks)
                dst = slot(i)[:, 0:k * n].rearrange("p (k n) -> p k n", k=k)
                src = w.rearrange("(k p) n -> p k n", p=P)[:, chunks[0]:chunks[0] + k, lo:lo + n]
                load(i, [(dst[:, 0:k // 2], src[:, 0:k // 2]), (dst[:, k // 2:], src[:, k // 2:])])

            def pair(i, w1, w3, lo, n):
                dst = slot(i).rearrange("p (m k n) -> p m k n", m=2, k=DC)
                load(i, [(dst[:, m], w.rearrange("(k p) n -> p k n", p=P)[:, :, lo:lo + n])
                         for m, w in enumerate((w1, w3))])

            for n in range(12):
                columns(S_MOD[0] + n, a["ev_mod_w"][0], 512 * n, 512)
            for n in range(4):
                columns(S_IN_E + n, a["ev_w_in"][0], 512 * n, 512)
            for n in range(2):
                columns(S_OUT_E + n, a["ev_w_out"][0], 512 * n, 512)
            if stop <= 6:
                return
            for n in range(UP_SLOTS):
                pair(S_UP + n, a["ev_ffn_w1"][0], a["ev_ffn_w3"][0], 256 * n, 256)
            for half in range(2):
                k0 = 0
                for j, k in enumerate(DOWN_SLOTS):
                    columns(S_DOWN + 3 * half + j, a["ev_ffn_w2"][0], 512 * half, 512, range(k0, k0 + k))
                    k0 += k
            for n in range(12):
                columns(S_MOD[1] + n, a["od_mod_w"][0], 512 * n, 512)
            for n, (lo_, w_) in enumerate(IN_COLS):
                columns(S_IN_O + n, a["od_w_in"][0], lo_, w_)
            for n in range(2):
                columns(S_OUT_O + n, a["od_w_out"][0], 512 * n, 512)
            if stop <= 14:
                return

            def expert_slot(e, p, b, c, rnd, wait):
                i = S_MOE + E_SLOTS * b + c
                if wait:
                    cp, bp = (c - RING, b) if c >= RING else (c - RING + E_SLOTS, b - 1)
                    n0 = (NE * rnd + 2 * p + bp)
                    if cp < W13_SLOTS:
                        sp.wait_ge(e_up, n0 * W13_SLOTS + cp + 1)
                    else:
                        sp.wait_ge(e_down, n0 * W2_SLOTS + cp - W13_SLOTS + 1)
                    sp.sem_inc(slots_reused, 1)
                dst = ring[:, i % RING, :]
                if c < W13_SLOTS:
                    dst = dst.rearrange("p (m k n) -> p m k n", m=2, k=DC)
                    for m, w in enumerate((a["od_exp_w1"], a["od_exp_w3"])):
                        sp.dma_start(dst[:, m], w[0, bass.ds(e, 1), :, 256 * c:256 * c + 256]
                                     .rearrange("o (k p) n -> p (o k) n", p=P)).then_inc(slot_landed[i % RING], 16)
                else:
                    r0 = 4 * P * (c - W13_SLOTS)
                    dst = dst.rearrange("p (k n) -> p k n", k=4)
                    src = a["od_exp_w2"][0, bass.ds(e, 1), r0:r0 + 4 * P, :].rearrange("o (k p) n -> p (o k) n", p=P)
                    for h in range(2):
                        sp.dma_start(dst[:, 2 * h:2 * h + 2], src[:, 2 * h:2 * h + 2]).then_inc(
                            slot_landed[i % RING], 16)

            def expert_weights(rnd):
                for c in range(RING):
                    if rnd == 0:
                        sp.wait_ge(*read(S_MOE - RING + c))
                    expert_slot(0, 0, 0, c, rnd, rnd > 0)
                with sp.Fori(0, NE // 2 - 1) as p:
                    for b in range(2):
                        for c in range(RING if b == 0 else 0, E_SLOTS):
                            expert_slot(2 * p + b, p, b, c, rnd, True)
                    for c in range(RING):
                        expert_slot(2 * p + 2, p + 1, 0, c, rnd, True)
                for b in range(2):
                    for c in range(RING if b == 0 else 0, E_SLOTS):
                        expert_slot(NE - 2 + b, NE // 2 - 1, b, c, rnd, True)

            expert_weights(0)
            sp.wait_ge(flag_ready, 1)
            crowded = sp.value_load(flag[0:1, 0:1], min_val=0, max_val=1)
            with sp.If(crowded > 0):
                expert_weights(1)
            for t in range(LAT_TILES):
                sp.wait_ge(final_ready, 2 * (t + 1))
                sp.dma_start(out[0, t * P:(t + 1) * P, :], X[:, t, :]).then_inc(out_done, 16)
            sp.wait_ge(out_done, 16 * LAT_TILES)

        @block.tensor
        def _(pe):
            def modulation(layer):
                if layer == 0:
                    pe.wait_ge(cond_ready, 1)
                    pe.wait_ge(cst_landed, 16)
                else:
                    pe.wait_ge(res_gated, 12)
                for n in range(13):
                    k = 12 * layer + n
                    if n < 12:
                        wait_slot(pe, S_MOD[layer] + n)
                        if k >= 2:
                            pe.wait_ge(mod_row, k - 1)
                        w = slot(S_MOD[layer] + n).rearrange("p (k n) -> p k n", k=DC)
                        for c in range(DC):
                            mm = pe.matmul(bank[4 * layer + k % 2][0:2, :], silc[:, c, :], w[:, c, :],
                                           start=(c == 0), stop=(c == DC - 1))
                        mm.then_inc(mod_psum, 1)
                    if n >= 1:
                        pe.wait_ge(mod_row, k)
                        for j in range(4):
                            col = 8 * (n - 1) + 2 * j
                            mm = pe.transpose(bank[4 * layer + 2][:, col:col + 2], mrow[0:2, (k - 1) % 2, j * P:(j + 1) * P],
                                              ident[0:2, 0:2])
                        if n == 12:
                            mm.then_inc(mod_turned, 1)

            def norm_turn(q):
                tiles = NORMS[q][3]
                pe.wait_ge(xn_ready, sum(NORMS[i][3] for i in range(q + 1)))
                for c in range(DC):
                    k = DC * q + c
                    if k >= 2:
                        pe.wait_ge(ht_act if k % 2 == 0 else ht_dve, k // 2)
                    for t in range(tiles):
                        mm = pe.transpose(bank[k % 2][:, t * P:(t + 1) * P], xn[:, t, c * P:(c + 1) * P], ident)
                    mm.then_inc(xn_turned, 1)

            def wait_ht(q):
                pe.wait_ge(ht_act, DC // 2 * (q + 1))
                pe.wait_ge(ht_dve, DC // 2 * (q + 1))

            def w_in_even():
                wait_ht(0)
                for j in range(16):
                    n, t = divmod(j, 4)
                    if t == 0:
                        wait_slot(pe, S_IN_E + n)
                    if j >= 4:
                        if (j - 4) // 4 in (0, 3):
                            pe.wait_ge(in_copied, j - 3)
                        else:
                            pe.wait_ge(in_normed, j - 4 - 3)
                    w = slot(S_IN_E + n).rearrange("p (k n) -> p k n", k=DC)
                    for c in range(DC):
                        mm = pe.matmul(bank[4 + j % 4][:, :], hT[:, c, t * P:(t + 1) * P], w[:, c, :],
                                       start=(c == 0), stop=(c == DC - 1))
                    mm.then_inc(in_psum, 1)

            def qk_turn_even():
                for j in range(8):
                    n, c = divmod(j, 4)
                    if c == 0:
                        pe.wait_ge(head_ready, 4 * (n + 1))
                    if j >= 2:
                        pe.wait_ge(qk_act if j % 2 == 0 else qk_dve, j // 2)
                    for t in range(TILES):
                        mm = pe.transpose(bank[j % 2][:, t * P:(t + 1) * P],
                                          hn[:, 1 + n, t, c * P:(c + 1) * P], ident)
                    mm.then_inc(qk_turned, 1)

            def fourier():
                pe.wait_ge(in_copied, 8)
                pe.wait_ge(in_normed, 8)
                pe.wait_ge(dft_landed, 16)
                for u in range(9):
                    if u < 8:
                        s, g = divmod(u, 4)
                        if u >= 2:
                            pe.wait_ge(four_t, u - 1)
                        for k in range(2):
                            mm = pe.matmul(bank[4 + u % 2][:, :], hn[:, 0, 2 * s + k, g * P:(g + 1) * P],
                                           dft[:, k * 512:(k + 1) * 512], start=(k == 0), stop=(k == 1))
                        mm.then_inc(four_a, 1)
                    if u >= 1:
                        v = u - 1
                        pe.wait_ge(four_t, v + 1)
                        if v >= 2:
                            pe.wait_ge(four_o, v - 1)
                        for k in range(2):
                            mm = pe.matmul(bank[6 + v % 2][:, 0:SEQ], dft[:, 1024 + k * P:1024 + (k + 1) * P],
                                           T1[:, v % 2, k * SEQ:(k + 1) * SEQ], start=(k == 0), stop=(k == 1))
                        mm.then_inc(four_b, 1)

            def attention(jobs, j0):
                n = len(jobs)
                for r in range(n + 2):
                    i = j0 + r
                    if r < n:
                        qa, ka, keys = jobs[r][0:3]
                        if i >= 3:
                            pe.wait_ge(exp_done, i - 2)
                        pe.matmul(bank[i % 3][:, 0:keys], qa, ka, start=True, stop=True).then_inc(scores, 1)
                    if 1 <= r <= n:
                        keys = jobs[r - 1][2]
                        pe.wait_ge(prob_ready, i)
                        if i >= 3:
                            pe.wait_ge(pt_ready, i - 2)
                        for k in range(keys // P):
                            mm = pe.transpose(bank[3 + (i - 1) % 2][:, k * P:(k + 1) * P],
                                              prob[:, (i - 1) % 3, k * P:(k + 1) * P], ident)
                        mm.then_inc(prob_turned, 1)
                    if r >= 2 and r % 2 == 1:
                        pe_pv(jobs, r - 2, i - 2)

            def pe_pv(jobs, r, i):
                keys, vs, half = jobs[r][2], jobs[r][3], jobs[r][4]
                pe.wait_ge(pt_ready, i + 1)
                h = i // 2
                if h >= 2:
                    pe.wait_ge(o_ready, h - 1)
                for k in range(keys // P):
                    mm = pe.matmul(bank[5 + h % 2][64 * half:64 * half + HD, 0:SEQ], vs[k], pT[:, h % 2, k, :],
                                   start=(k == 0), stop=(k == keys // P - 1))
                mm.then_inc(o_psum, 1)

            def gate_rows(q):
                layer, m, streams = GATES[q]
                k = 2 * sum(GATES[i][2] for i in range(q))
                for s in range(streams):
                    for half in range(2):
                        if k >= 1:
                            pe.wait_ge(gate_ready, k)
                        else:
                            pe.wait_ge(four_o, 8)
                        for j in range(4):
                            c = m + 4 * half + j
                            mm = pe.matmul(bank[7][:, j * P:(j + 1) * P],
                                           mod[layer][:, c, s:s + 1].to_broadcast([P, P]), ident,
                                           start=True, stop=True)
                        mm.then_inc(gate_psum, 1)
                        k += 1

            def w_out(slot0, tiles, oTv, r0):
                for half in range(2):
                    wait_slot(pe, slot0 + half)
                    w = slot(slot0 + half).rearrange("p (k n) -> p k n", k=DC)
                    for t in range(tiles):
                        r = r0 + half * tiles + t
                        if half * tiles + t >= 4:
                            pe.wait_ge(res_gated, r - 3)
                        for c in range(DC):
                            mm = pe.matmul(bank[3 + (half * tiles + t) % 4][:, :], oTv[:, c, t * P:(t + 1) * P],
                                           w[:, c, :], start=(c == 0), stop=(c == DC - 1))
                        mm.then_inc(res_psum, 1)

            def ffn_up():
                wait_ht(1)
                for f in range(FC):
                    n, half = divmod(f, 2)
                    if half == 0:
                        wait_slot(pe, S_UP + n)
                    if f >= 2:
                        pe.wait_ge(up_gated, f - 1)
                    w = slot(S_UP + n).rearrange("p (m k n) -> p m k n", m=2, k=DC)
                    for m in range(2):
                        for c in range(DC):
                            mm = pe.matmul(bank[2 * (f % 2) + m][:, :], w[:, m, c, half * P:(half + 1) * P],
                                           hT[:, c, :], start=(c == 0), stop=(c == DC - 1))
                    mm.then_inc(up_psum, 1)

            def ffn_down(r0):
                for half in range(2):
                    k0 = 0
                    b0 = 4 if half == 0 else 0
                    for j, ks in enumerate(DOWN_SLOTS):
                        wait_slot(pe, S_DOWN + 3 * half + j)
                        w = slot(S_DOWN + 3 * half + j)[:, 0:ks * 512].rearrange("p (k n) -> p k n", k=ks)
                        for k in range(ks):
                            kk = k0 + k
                            if half == 0:
                                pe.wait_ge(up_gated, kk + 1)
                            elif kk == 0:
                                pe.wait_ge(up_gated, FC)
                            for t in range(TILES):
                                mm = pe.matmul(bank[b0 + t][:, :], gT[:, kk, t * P:(t + 1) * P], w[:, k, :],
                                               start=(kk == 0), stop=(kk == FC - 1))
                                if kk == FC - 1:
                                    mm.then_inc(res_psum, 1)
                        if j < 2:
                            mm.then_inc(down_read, 1)
                        k0 += ks

            modulation(0)
            if stop <= 1:
                return
            norm_turn(0)
            w_in_even()
            qk_turn_even()
            if stop <= 3:
                return
            fourier()
            pe.wait_ge(qk_act, 4)
            pe.wait_ge(qk_dve, 4)
            attention(EVEN_JOBS, 0)
            if stop <= 4:
                return
            gate_rows(0)
            pe.wait_ge(o_ready, len(EVEN_JOBS) // 2)
            pe.wait_ge(four_o, 8)
            w_out(S_OUT_E, 4, oT, 0)
            norm_turn(1)
            gate_rows(1)
            if stop <= 6:
                return
            ffn_up()
            ffn_down(8)
            if stop <= 8:
                return

            def w_in_odd():
                wait_ht(2)
                for i, (n, t) in enumerate(IN_JOBS):
                    if t == 0:
                        wait_slot(pe, S_IN_O + n)
                    if i >= 4:
                        pe.wait_ge(*((in_normed, i + 5) if i - 4 < 8 else (in_copied, i + 1)))
                    w_ = IN_COLS[n][1]
                    w = slot(S_IN_O + n)[:, 0:DC * w_].rearrange("p (k n) -> p k n", k=DC)
                    for c in range(DC):
                        mm = pe.matmul(bank[4 + i % 4][:, 0:w_], hT[:, c, t * P:(t + 1) * P], w[:, c, :],
                                       start=(c == 0), stop=(c == DC - 1))
                    mm.then_inc(in_psum, 1)

            def turn_odd():
                for jj in range(10):
                    j = 8 + jj
                    if jj == 0:
                        pe.wait_ge(head_ready, 12)
                    if jj == 3:
                        pe.wait_ge(head_ready, 16)
                    if jj == 6:
                        pe.wait_ge(in_copied, 16)
                    pe.wait_ge(qk_act if j % 2 == 0 else qk_dve, j // 2)
                    for t in range(4):
                        o = bank[j % 2][:, t * P:(t + 1) * P]
                        if jj < 3:
                            mm = pe.transpose(o, qn[:, t % 2, (2 * jj + t // 2) * P:(2 * jj + t // 2 + 1) * P], ident)
                        elif jj < 6:
                            mm = pe.transpose(o, kn[:, t, jj - 3, :, :].rearrange("p b d -> p (b d)"), ident)
                        elif jj < 8:
                            mm = pe.transpose(o, un[:, (t + 2) % 4, (jj - 6) * P:(jj - 5) * P], ident)
                        else:
                            mm = pe.matmul(o, un[:, 3 - t, (jj - 8) * P:(jj - 7) * P], rev,
                                           start=True, stop=True)
                    mm.then_inc(qk_turned, 1)

            def s5():
                pe.wait_ge(s5_bbar, 1)
                pe.wait_ge(in_normed, 16)
                for i in range(2):
                    for g in range(4):
                        mm = pe.transpose(bank[2 + i][:, g * P:(g + 1) * P],
                                          b_bar[i][:, 4 * g:4 * g + 4, :].rearrange("p u n -> p (u n)"), ident)
                    mm.then_inc(s5_turned, 1)
                pe.wait_ge(s5_bt_act, 1)
                pe.wait_ge(s5_bt_dve, 1)
                pe.wait_ge(qk_act, 9)
                pe.wait_ge(qk_dve, 9)
                pe.wait_ge(s5_c, 1)
                for k in range(UNITS + 1):
                    if k < UNITS:
                        j, d = divmod(k, 2)
                        g, r = 2 * d + j // 4, 32 * (j % 4)
                        if k >= 2:
                            pe.wait_ge(s5_bu_used, k - 1)
                        for i in range(2):
                            mm = pe.matmul(bank[2 * (k % 2) + i][:, :], BT[i][r:r + 32, g * P:(g + 1) * P],
                                           uT[d][r:r + 32, j // 4, :], start=True, stop=True)
                        mm.then_inc(s5_bu, 1)
                    if k >= 1:
                        j, d = divmod(k - 1, 2)
                        r, u = 32 * (j % 4), PAIRS * d + j
                        pe.wait_ge(s5_s, k)
                        for i in range(2):
                            mm = pe.matmul(bank[4 + j // 4][r:r + 32, 0:SEQ], C5[i][:, u, :],
                                           s_out[:, (k - 1) % 2, i, :], start=(d == 0 and i == 0),
                                           stop=(d == 1 and i == 1))
                        mm.then_inc(s5_y, 1)
                pe.wait_ge(glu_landed, 16)
                pe.wait_ge(y5_gelu, 1)
                for m in range(2):
                    for k in range(2):
                        mm = pe.matmul(bank[6][:, m * SEQ:(m + 1) * SEQ], gluw[:, k, m * P:(m + 1) * P], y5s[:, k, :],
                                       start=(k == 0), stop=(k == 1))
                mm.then_inc(glu_psum, 1)

            modulation(1)
            norm_turn(2)
            w_in_odd()
            turn_odd()
            if stop <= 10:
                return
            s5()
            if stop <= 11:
                return
            pe.wait_ge(ssm_ready, 1)
            attention(ODD_JOBS, ATTN_E)
            if stop <= 12:
                return
            gate_rows(2)
            pe.wait_ge(o_ready, len(EVEN_JOBS) // 2 + len(ODD_JOBS) // 2)
            w_out(S_OUT_O, 2, oTo, 16)
            norm_turn(3)
            gate_rows(3)
            if stop <= 14:
                return

            wait_ht(3)
            for t in range(2):
                for c in range(DC):
                    mm = pe.matmul(bank[2][:, 8 * t:8 * t + 8], hT[:, c, t * P:(t + 1) * P],
                                   vec[:, V_RW + 8 * c:V_RW + 8 * c + 8], start=(c == 0), stop=(c == DC - 1))
            mm.then_inc(logits, 1)
            pe.wait_ge(sel_ready, 1)
            tri, one = cst[:, C_TRI:C_TRI + P], cst[:, C_ONE:C_ONE + P]
            sel = s5v[:, R_SEL, :]
            for o, parts in ((0, [(tri, 0)]), (8, [(one, 0), (tri, 1)]), (16, [(one, 0), (one, 1)])):
                for k, (m, t) in enumerate(parts):
                    mm = pe.matmul(bank[3][:, o:o + 8], m, sel[:, 8 * t:8 * t + 8], start=(k == 0),
                                   stop=(k == len(parts) - 1))
            mm.then_inc(ranks, 1)

            def gather(e, n, b):
                pe.wait_ge(e_added, 4 * n)
                for h in range(2):
                    for j in range(4):
                        c = 4 * h + j
                        for t in range(2):
                            mm = pe.matmul(bank[6 + h][:, j * P:(j + 1) * P], xn[:, t, c * P:(c + 1) * P],
                                           pick[:, t, bass.ds(e, 1), :].rearrange("p o s -> p (o s)"),
                                           start=(t == 0), stop=(t == 1))
                    mm.then_inc(e_gather, 1)

            def turn_hidden(n, m):
                pe.wait_ge(e_gated, 2 + W13_SLOTS * n + m + 1)
                pe.wait_ge(e_heT, W13_SLOTS * n + m + 1)
                for j in range(2):
                    mm = pe.transpose(bank[2 + m % 2][:, j * P:(j + 1) * P], he[:, m % 2, j * P:(j + 1) * P], ident)
                mm.then_inc(e_turned, 1)

            def expert(p, b, rnd):
                e = 2 * p + b
                n = e + NE * rnd
                i0 = S_MOE + E_SLOTS * b
                pe.wait_ge(xe_act, n + 1 + rnd)
                pe.wait_ge(xe_dve, n + 1 + rnd)
                for m in range(W13_SLOTS):
                    i = i0 + m
                    pe.wait_ge(slot_landed[i % RING], 32 * (i // RING + 1) + (p + 4 * rnd) * (32 * 2 * E_SLOTS // RING))
                    pe.wait_ge(e_gated, W13_SLOTS * n + m + 1)
                    w = ring[:, i % RING, :].rearrange("p (m k n) -> p k m n", m=2, k=DC)
                    for c in range(DC):
                        mm = pe.matmul(bank[m % 2][:, :], xe[:, b, c, :], w[:, c], start=(c == 0), stop=(c == DC - 1))
                    mm.then_inc(e_up, 1)
                    if m >= 1:
                        turn_hidden(n, m - 1)
                turn_hidden(n, W13_SLOTS - 1)
                for s_ in range(W2_SLOTS):
                    i = i0 + W13_SLOTS + s_
                    pe.wait_ge(slot_landed[i % RING], 32 * (i // RING + 1) + (p + 4 * rnd) * (32 * 2 * E_SLOTS // RING))
                    w = ring[:, i % RING, :].rearrange("p (k n) -> p k n", k=4)
                    for k in range(4):
                        c = 4 * s_ + k
                        if k % 2 == 0:
                            pe.wait_ge(e_heT, 2 + W13_SLOTS * n + c // 2 + 1)
                        for h in range(2):
                            mm = pe.matmul(bank[4 + h][:, :], heT[:, c, :], w[:, k, h * 512:(h + 1) * 512],
                                           start=(c == 0), stop=(c == EC - 1))
                    mm.then_inc(e_down, 1)
                gather(e + 1, n, 1 - b)
                pe.wait_ge(y_act, n + 1)
                pe.wait_ge(y_dve, n + 1)
                pe.wait_ge(gte_ready, n + 1)
                for k in range(4):
                    h, t = divmod(k, 2)
                    if k < 2:
                        pe.wait_ge(xe_act if k == 0 else xe_dve, n + 2 + rnd)
                    else:
                        pe.wait_ge(e_added, 4 * n + k - 1)
                    pe.matmul(bank[6 + k % 2][:, :], gTe[:, b, t * P:(t + 1) * P], ye[:, h * 512:(h + 1) * 512],
                              start=True, stop=True).then_inc(e_scatter, 1)

            def experts(rnd):
                pe.wait_ge(pick_ready, rnd + 1)
                if rnd == 0:
                    pe.wait_ge(gate_ready, 12)
                for g in range(4):
                    for j in range(2):
                        for t in range(2):
                            mm = pe.transpose(bank[2 + g][:, (2 * j + t) * P:(2 * j + t + 1) * P],
                                              gpick[:, t, 2 * g + j, :], ident)
                    mm.then_inc(gpick_turned, 1)
                pe.wait_ge(gta_act, 2 * (rnd + 1))
                pe.wait_ge(gta_dve, 2 * (rnd + 1))
                gather(0, NE * rnd, 0)
                with pe.Fori(0, NE // 2) as p:
                    for b in range(2):
                        expert(p, b, rnd)

            experts(0)
            pe.wait_ge(flag_ready, 1)
            crowded = pe.value_load(flag[0:1, 0:1], min_val=0, max_val=1)
            with pe.If(crowded > 0):
                experts(1)

        @block.scalar
        def _(act):
            act.dma_start(vec[:, :], a["vec"]).then_inc(vec_landed, 16)
            act.dma_start(cst[:, :], a["cst"]).then_inc(cst_landed, 16)
            act.dma_start(X[:, 0:2, :], a["x"][0].rearrange("(t p) d -> p t d", p=P)).then_inc(x_landed, 16)
            act.dma_start(X[:, 2:4, :], a["ctx"][0].rearrange("(t p) d -> p t d", p=P)).then_inc(x_landed, 16)
            act.dma_start(dft, a["dft"]).then_inc(dft_landed, 16)
            act.wait_ge(vec_landed, 16)
            act.activation(silc[:, :, :], vec[:, V_COND:V_COND + 16].rearrange("p (k s) -> p k s", s=2),
                           ACT.Silu).then_inc(cond_ready, 1)

            roots = [0]

            def root(v):
                roots[0] += 1
                act.wait_ge(mean_ready, roots[0])
                act.activation(v, v, ACT.Sqrt).then_inc(root_ready, 1)

            def squares(q):
                tiles, before = NORMS[q][3:5]
                if q == 0:
                    act.wait_ge(x_landed, 32)
                else:
                    act.wait_ge(res_done, before)
                for t in range(tiles):
                    act.activation(xn[:, t, :], X[:, t, :], ACT.Square,
                                   accum_out=ss[:, t:t + 1]).then_inc(square_sum, 1)
                root(rstd[:, 0:tiles])

            def modulate(q):
                layer, sh, sc = NORMS[q][0:3]
                act.wait_ge(coef_ready, q + 1)
                for c in range(0, DC, 2):
                    act.wait_ge(xn_turned, DC * q + c + 1)
                    for s in range(NORMS[q][3] // 2):
                        ins = act.activation(hT[:, c, s * SEQ:(s + 1) * SEQ], bank[0][:, s * SEQ:(s + 1) * SEQ],
                                             ACT.Identity, bias=mod[layer][:, sh + c, s:s + 1],
                                             scale=coef[:, q, c, s:s + 1])
                    ins.then_inc(ht_act, 1)

            squares(0)
            if stop <= 1:
                return
            modulate(0)
            for j in range(16):
                n, t = divmod(j, 4)
                act.wait_ge(in_psum, j + 1)
                if n in (0, 3):
                    act.activation(hn[:, n, t, :], bank[4 + j % 4][:, :], ACT.Copy).then_inc(in_copied, 1)
                else:
                    if j - 4 >= 2:
                        act.wait_ge(in_summed, j - 5)
                    act.activation(sq[:, j % 2, :], bank[4 + j % 4][:, :], ACT.Square).then_inc(in_squared, 1)
                    root(hss[:, 0:8])
            for j in range(0, 8, 2):
                act.wait_ge(qk_turned, j + 1)
                act.activation(hT[:, j, :], bank[0][:, :], ACT.Copy).then_inc(qk_act, 1)
            if stop <= 3:
                return
            for u in range(8):
                act.wait_ge(four_a, u + 1)
                if u >= 2:
                    act.wait_ge(four_b, u - 1)
                act.activation(T1[:, u % 2, :], bank[4 + u % 2][:, :], ACT.Copy).then_inc(four_t, 1)

            def attention(jobs, j0):
                n = len(jobs)
                for r in range(n + 2):
                    i = j0 + r
                    if r < n:
                        keys = jobs[r][2]
                        act.wait_ge(row_max, i + 1)
                        if i >= 3:
                            act.wait_ge(prob_turned, i - 2)
                        act.activation(prob[:, i % 3, 0:keys], bank[i % 3][:, 0:keys], ACT.Exp,
                                       bias=nmax[:, i % 4:i % 4 + 1],
                                       accum_out=rsum[:, i % 4:i % 4 + 1]).then_inc(exp_done, 1)
                    if r >= 2:
                        keys = jobs[r - 2][2]
                        k = i - 2
                        act.wait_ge(prob_turned, k + 1)
                        if k // 2 >= 2:
                            act.wait_ge(o_psum, k // 2 - 1)
                        act.activation(pT[:, (k // 2) % 2, 0:keys // P, (k % 2) * P:(k % 2 + 1) * P],
                                       bank[3 + k % 2][:, 0:keys].rearrange("p (k q) -> p k q", q=P),
                                       ACT.Copy).then_inc(pt_ready, 1)

            def gate_rows(q):
                layer, m, streams = GATES[q]
                k = 2 * sum(GATES[i][2] for i in range(q))
                if q:
                    act.wait_ge(res_gated, [0, 8, 16, 20][q])
                if q % 2 == 0:
                    act.wait_ge(prob_turned, len(EVEN_JOBS) + (len(ODD_JOBS) if q else 0))
                for s in range(streams):
                    for half in range(2):
                        act.wait_ge(gate_psum, k + 1)
                        g = G2 if q == 3 else G[:, s, :]
                        act.activation(g[:, half * 512:(half + 1) * 512], bank[7][:, :],
                                       ACT.Copy).then_inc(gate_ready, 1)
                        k += 1

            attention(EVEN_JOBS, 0)
            if stop <= 4:
                return
            gate_rows(0)
            squares(1)
            modulate(1)
            gate_rows(1)
            if stop <= 6:
                return
            for f in range(FC):
                act.wait_ge(up_psum, f + 1)
                if f >= 2:
                    act.wait_ge(up_gated, f - 1)
                act.activation(sil[:, f % 2, :], bank[2 * (f % 2)][:, :], ACT.Silu).then_inc(up_silu, 1)
            if stop <= 8:
                return
            act.wait_ge(four_b, 8)
            act.dma_start(S[:, 5120:6144].rearrange("p (i n) -> p i n", i=2),
                          a["s5b"].rearrange("i p n -> p i n")).then_inc(s5_raw, 16)
            act.wait_ge(res_psum, 16)
            act.dma_start(B[:, 9984:11008].rearrange("p (i n) -> p i n", i=2),
                          a["s5c"].rearrange("i p n -> p i n")).then_inc(s5_raw, 16)
            squares(2)
            modulate(2)
            for i, (n, t) in enumerate(IN_JOBS):
                act.wait_ge(in_psum, 16 + i + 1)
                ps = bank[4 + i % 4]
                if n == 3:
                    act.activation(un[:, t, :], ps[:, 0:256], ACT.Copy).then_inc(in_copied, 1)
                    continue
                w_ = (512, 256, 192)[n]
                if i < 2:
                    act.wait_ge(in_summed, 8)
                else:
                    act.wait_ge(in_summed, 8 + i - 1)
                act.activation(sq[:, i % 2, 0:w_], ps[:, 0:w_], ACT.Square).then_inc(in_squared, 1)
                if n == 2:
                    act.activation(vn[:, t, :], ps[:, 192:384], ACT.Copy).then_inc(in_copied, 1)
                root(hss[:, 0:w_ // HD])
            for j in range(8, 18, 2):
                act.wait_ge(qk_turned, j + 1)
                jj = j - 8
                dst = (HT[:, 512 * jj:512 * jj + 512] if jj < 6 else uT[(jj - 6) // 2][:, jj % 2, :])
                act.activation(dst, bank[0][:, :], ACT.Copy).then_inc(qk_act, 1)
            if stop <= 10:
                return
            act.dma_start(gluw, a["od_s5_glu_w"][0].rearrange("(k p) n -> p k n", p=P)).then_inc(glu_landed, 16)
            act.wait_ge(s5_turned, 1)
            act.activation(BT[0], bank[2][:, :], ACT.Copy).then_inc(s5_bt_act, 1)
            act.wait_ge(y5_ready, 1)
            act.activation(y5s[:, :, :], y5[:, :, :], ACT.Gelu_apprx_tanh).then_inc(y5_gelu, 1)
            act.wait_ge(glu_psum, 1)
            for m in range(2):
                ins = act.activation(y5[:, m, :], bank[6][:, m * SEQ:(m + 1) * SEQ], ACT.Sigmoid,
                                     bias=vec[:, V_GLUB + m:V_GLUB + m + 1])
            ins.then_inc(glu_sig, 1)
            if stop <= 11:
                return
            attention(ODD_JOBS, ATTN_E)
            if stop <= 12:
                return
            gate_rows(2)
            squares(3)
            modulate(3)
            gate_rows(3)
            if stop <= 14:
                return
            act.wait_ge(top_gap, 1)
            act.activation(s5v[:, R_T, 4:6], s5v[:, R_T, 2:4], ACT.Exp).then_inc(top_exp, 1)

            def gathered(n, b):
                act.wait_ge(e_gather, 2 * n + 1)
                for c in range(4):
                    ins = act.activation(xe[:, b, c, :], bank[6][:, c * P:(c + 1) * P], ACT.Identity,
                                         bias=mod[1][:, M_SH2 + c, 0:1], scale=coef[:, 3, c, 0:1])
                ins.then_inc(xe_act, 1)

            def turned(n, m):
                act.wait_ge(e_turned, W13_SLOTS * n + m + 1)
                act.activation(heT[:, 2 * m:2 * m + 2, :], bank[2 + m % 2][:, 0:2 * P]
                               .rearrange("p (c s) -> p c s", c=2), ACT.Copy).then_inc(e_heT, 1)

            def experts(rnd):
                for g in range(0, 4, 2):
                    act.wait_ge(gpick_turned, 4 * rnd + g + 1)
                    act.activation(gTall[:, 2 * g:2 * g + 2, :].rearrange("p e t -> p (e t)"), bank[2 + g][:, :],
                                   ACT.Copy).then_inc(gta_act, 1)
                gathered((NE + 1) * rnd, 0)
                with act.Fori(0, NE // 2) as p:
                    for b in range(2):
                        n = 2 * p + b + NE * rnd
                        for m in range(W13_SLOTS):
                            act.wait_ge(e_up, W13_SLOTS * n + m + 1)
                            act.activation(sile[:, m % 2, :], bank[m % 2][:, 0:256], ACT.Silu).then_inc(e_silu, 1)
                            if m >= 1:
                                turned(n, m - 1)
                        turned(n, W13_SLOTS - 1)
                        act.wait_ge(e_down, W2_SLOTS * (n + 1))
                        act.activation(ye[:, 0:512], bank[4][:, :], ACT.Copy).then_inc(y_act, 1)
                        gathered(n + rnd + 1, 1 - b)

            act.sem_inc(e_heT, 2)
            experts(0)
            act.wait_ge(flag_ready, 1)
            crowded = act.value_load(flag[0:1, 0:1], min_val=0, max_val=1)
            with act.If(crowded > 0):
                experts(1)

        @block.vector
        def _(dve):
            steps = [0]

            def step(ins):
                steps[0] += 1
                ins.then_inc(dve_step, 1)
                dve.wait_ge(dve_step, steps[0])

            roots = [0]

            def rsqrt_mean(o, sums, n):
                roots[0] += 1
                dve.tensor_scalar(o, sums, 1.0 / n, EPS, ALU.mult, ALU.add).then_inc(mean_ready, 1)
                dve.wait_ge(root_ready, roots[0])
                step(dve.reciprocal(o, o))

            def modulation(layer):
                for n in range(12):
                    k = 12 * layer + n
                    dve.wait_ge(mod_psum, k + 1)
                    dve.tensor_copy(mrow[0:2, k % 2, :], bank[4 * layer + k % 2][0:2, :]).then_inc(mod_row, 1)
                dve.wait_ge(mod_turned, layer + 1)
                b = vec[:, V_MODB + 48 * layer:V_MODB + 48 * layer + 48]
                step(dve.tensor_tensor(mod[layer][:, :, :], bank[4 * layer + 2][:, 0:96].rearrange("p (c s) -> p c s", s=2),
                                       b.unsqueeze(2).to_broadcast([P, 48, 2]), ALU.add))
                for q in (2 * layer, 2 * layer + 1):
                    sc = NORMS[q][2]
                    gain = vec[:, V_NORM + DC * q:V_NORM + DC * q + DC]
                    step(dve.tensor_scalar(coef[:, q], mod[layer][:, sc:sc + DC, :], 1.0, None, ALU.add))
                    dve.tensor_tensor(coef[:, q], coef[:, q], gain.unsqueeze(2).to_broadcast([P, DC, 2]),
                                      ALU.mult).then_inc(coef_ready, 1)
                dve.wait_ge(coef_ready, 2 * layer + 2)

            def normed(q):
                tiles = NORMS[q][3]
                dve.wait_ge(square_sum, sum(NORMS[i][3] for i in range(q + 1)))
                rsqrt_mean(rstd[:, 0:tiles], ss[:, 0:tiles], D)
                for t in range(tiles):
                    dve.tensor_scalar(xn[:, t, :], X[:, t, :], rstd[:, t:t + 1], None,
                                      ALU.mult).then_inc(xn_ready, 1)

            def modulate(q):
                layer, sh = NORMS[q][0:2]
                for c in range(1, DC, 2):
                    dve.wait_ge(xn_turned, DC * q + c + 1)
                    for s in range(NORMS[q][3] // 2):
                        ins = dve.tensor_scalar(hT[:, c, s * SEQ:(s + 1) * SEQ], bank[1][:, s * SEQ:(s + 1) * SEQ],
                                                coef[:, q, c, s:s + 1], mod[layer][:, sh + c, s:s + 1],
                                                ALU.mult, ALU.add)
                    ins.then_inc(ht_dve, 1)

            def gated_sum(half_tiles, r0, banks):
                for k, (half, t) in enumerate(half_tiles):
                    r = r0 + k
                    dve.wait_ge(res_psum, r + 1)
                    if k == 0:
                        dve.wait_ge(gate_ready, {0: 4, 8: 8, 16: 10, 20: 12}[r0])
                    if r >= 2:
                        dve.wait_ge(res_done, r - 1)
                    dve.tensor_tensor(tmp[:, r % 2, :], bank[banks[k]][:, :],
                                      G[:, t // 2, half * 512:(half + 1) * 512], ALU.mult).then_inc(res_gated, 1)

            dve.wait_ge(vec_landed, 16)
            are, aim = vec[:, V_ARE:V_ARE + 16], vec[:, V_AIM:V_AIM + 16]
            dve.tensor_tensor(s5v[:, 1, :], are, are, ALU.mult)
            step(dve.tensor_tensor(s5v[:, 2, :], aim, aim, ALU.mult))
            step(dve.tensor_tensor(s5v[:, 1, :], s5v[:, 1, :], s5v[:, 2, :], ALU.add))
            dve.reciprocal(s5v[:, 1, :], s5v[:, 1, :]).then_inc(s5_rden, 1)
            for hg in (H_EQ, H_OQ):
                g = vec[:, V_HEAD + hg * HD:V_HEAD + (hg + 1) * HD]
                step(dve.tensor_scalar(g, g, HD ** -0.5, None, ALU.mult))
            normed(0)
            modulation(0)
            if stop <= 1:
                return
            modulate(0)
            for j in range(4, 12):
                n, t = divmod(j, 4)
                dve.wait_ge(in_squared, j - 3)
                dve.tensor_reduce(hss[:, 0:8], sq[:, j % 2, :].rearrange("p (h d) -> p h d", d=HD), AX,
                                  ALU.add).then_inc(in_summed, 1)
                dve.wait_ge(in_summed, j - 3)
                rsqrt_mean(hss[:, 0:8], hss[:, 0:8], HD)
                dve.tensor_tensor(hn[:, n, t, :].rearrange("p (h d) -> p h d", d=HD),
                                  bank[4 + j % 4][:, :].rearrange("p (h d) -> p h d", d=HD),
                                  hss[:, 0:8].unsqueeze(2).to_broadcast([P, 8, HD]), ALU.mult).then_inc(in_normed, 1)
                dve.wait_ge(in_normed, j - 3)
            for j in range(1, 8, 2):
                dve.wait_ge(qk_turned, j + 1)
                dve.tensor_copy(hT[:, j, :], bank[1][:, :]).then_inc(qk_dve, 1)
            if stop <= 3:
                return
            for u in range(8):
                s, g = divmod(u, 4)
                dve.wait_ge(four_b, u + 1)
                if u == 0:
                    dve.wait_ge(qk_turned, 8)
                dve.tensor_copy(oT[:, g, s * SEQ:(s + 1) * SEQ], bank[6 + u % 2][:, 0:SEQ]).then_inc(four_o, 1)

            def attention(jobs, j0, oTv, c0):
                n = len(jobs)
                for r in range(n + 2):
                    i = j0 + r
                    if r < n:
                        keys, h, s = jobs[r][2], jobs[r][5], jobs[r][6]
                        sc = bank[i % 3]
                        dve.wait_ge(scores, i + 1)
                        if jobs is EVEN_JOBS and s == 0:
                            dve.wait_ge(bias_ready, h + 1)
                            dve.tensor_tensor(sc[:, 0:SEQ], sc[:, 0:SEQ], bias[:, h % 2, (r % 2) * SEQ:(r % 2 + 1) * SEQ],
                                              ALU.add).then_inc(bias_used, 1)
                            dve.wait_ge(bias_used, i + 1)
                        if i >= 4:
                            dve.wait_ge(exp_done, i - 3)
                        dve.tensor_reduce(nmax[:, i % 4:i % 4 + 1], sc[:, 0:keys], AX, ALU.max,
                                          negate=True).then_inc(row_max, 1)
                    if 1 <= r <= n:
                        k = i - 1
                        keys = jobs[r - 1][2]
                        dve.wait_ge(exp_done, k + 1)
                        step(dve.reciprocal(rinv[:, k % 4:k % 4 + 1], rsum[:, k % 4:k % 4 + 1]))
                        dve.tensor_scalar(prob[:, k % 3, 0:keys], prob[:, k % 3, 0:keys], rinv[:, k % 4:k % 4 + 1],
                                          None, ALU.mult).then_inc(prob_ready, 1)
                    if r >= 3 and r % 2 == 1:
                        head_out(jobs, (r - 3) // 2, (i - 3) // 2, oTv, c0)

            def head_out(jobs, hr, h, oTv, c0):
                half, head, s = jobs[2 * hr][4:7]
                dve.wait_ge(o_psum, h + 1)
                dve.tensor_copy(oTv[64 * half:64 * half + HD, c0 + head // 2, s * SEQ:(s + 1) * SEQ],
                                bank[5 + h % 2][64 * half:64 * half + HD, 0:SEQ]).then_inc(o_ready, 1)

            attention(EVEN_JOBS, 0, oT, 4)
            if stop <= 4:
                return
            halves4 = [(half, t) for half in range(2) for t in range(4)]
            gated_sum(halves4, 0, [3 + k % 4 for k in range(8)])
            normed(1)
            modulate(1)
            if stop <= 6:
                return
            for f in range(FC):
                dve.wait_ge(up_silu, f + 1)
                dve.tensor_tensor(gT[:, f, :], sil[:, f % 2, :], bank[2 * (f % 2) + 1][:, :],
                                  ALU.mult).then_inc(up_gated, 1)
            gated_sum(halves4, 8, [4, 5, 6, 7, 0, 1, 2, 3])
            if stop <= 8:
                return
            dve.wait_ge(s5_raw, 32)
            dve.tensor_scalar(C5[1], C5[1], -1.0, None, ALU.mult).then_inc(s5_c, 1)
            normed(2)
            modulation(1)
            modulate(2)
            for i, (n, t) in enumerate(IN_JOBS[:8]):
                heads = (8, 4, 3)[n]
                w_ = heads * HD
                dve.wait_ge(in_squared, 8 + i + 1)
                dve.tensor_reduce(hss[:, 0:heads], sq[:, i % 2, 0:w_].rearrange("p (h d) -> p h d", d=HD), AX,
                                  ALU.add).then_inc(in_summed, 1)
                dve.wait_ge(in_summed, 8 + i + 1)
                rsqrt_mean(hss[:, 0:heads], hss[:, 0:heads], HD)
                dst = (kn[:, t, :, 0, :] if n == 2 else
                       qn[:, t, 512 * n:512 * n + w_].rearrange("p (h d) -> p h d", d=HD))
                dve.tensor_tensor(dst, bank[4 + i % 4][:, 0:w_].rearrange("p (h d) -> p h d", d=HD),
                                  hss[:, 0:heads].unsqueeze(2).to_broadcast([P, heads, HD]),
                                  ALU.mult).then_inc(in_normed, 1)
                dve.wait_ge(in_normed, 8 + i + 1)
            for j in range(9, 18, 2):
                dve.wait_ge(qk_turned, j + 1)
                jj = j - 8
                dst = (HT[:, 512 * jj:512 * jj + 512] if jj < 6 else uT[(jj - 6) // 2][:, jj % 2, :])
                dve.tensor_copy(dst, bank[1][:, :]).then_inc(qk_dve, 1)
            if stop <= 10:
                return
            dve.wait_ge(s5_turned, 2)
            dve.tensor_copy(BT[1], bank[3][:, :]).then_inc(s5_bt_dve, 1)

            for k in range(UNITS):
                j, d = divmod(k, 2)
                u = PAIRS * d + j
                br, bi = bank[2 * (k % 2)][:, :], bank[2 * (k % 2) + 1][:, :]
                co, si = turn[:, k % 2, 0, :], turn[:, k % 2, 1, :]
                dve.wait_ge(s5_table, k + 1)
                dve.wait_ge(s5_bu, k + 1)
                if k:
                    dve.wait_ge(s5_s, k)
                dve.tensor_tensor(z[0], br, co, ALU.mult)
                step(dve.tensor_tensor(vt[0], bi, si, ALU.mult))
                dve.tensor_tensor(z[0], z[0], vt[0], ALU.add)
                dve.tensor_tensor(z[1], bi, co, ALU.mult)
                step(dve.tensor_tensor(vt[1], br, si, ALU.mult))
                dve.sem_inc(s5_bu_used, 1)
                step(dve.tensor_tensor(z[1], z[1], vt[1], ALU.subtract))
                r = s5v[:, S_R, u:u + 1].to_broadcast([P, TOK])
                for i in range(2):
                    ins = dve.tensor_tensor_scan(z[i], r, z[i], 0.0, ALU.mult, ALU.add)
                step(ins)
                if k >= 2:
                    dve.wait_ge(s5_y, k - 1)
                co, si, zr, zi = (x[:, SEQ:TOK] for x in (co, si, z[0], z[1]))
                vr, vi = vt[0][:, 0:SEQ], vt[0][:, SEQ:]
                wr, wi = vt[1][:, 0:SEQ], vt[1][:, SEQ:]
                dve.tensor_tensor(vr, zr, co, ALU.mult)
                dve.tensor_tensor(wr, zi, si, ALU.mult)
                dve.tensor_tensor(vi, zr, si, ALU.mult)
                step(dve.tensor_tensor(wi, zi, co, ALU.mult))
                o = [s_out[:, k % 2, i, :] if d == 0 else s_out[:, k % 2, i, ::-1] for i in range(2)]
                dve.tensor_tensor(o[0], vr, wr, ALU.subtract)
                dve.tensor_tensor(o[1], vi, wi, ALU.add).then_inc(s5_s, 1)
            dve.wait_ge(s5_y, UNITS)
            for m in range(2):
                ins = dve.scalar_tensor_tensor(out=y5[:, m, :], in0=uT[0][:, m, CTX:], scalar=vec[:, V_D + m:V_D + m + 1],
                                               in1=bank[4 + m][:, 0:SEQ], op0=ALU.mult, op1=ALU.add)
            ins.then_inc(y5_ready, 1)
            dve.wait_ge(glu_sig, 1)
            dve.tensor_tensor(oTo[:, 6:8, :], y5s[:, :, :], y5[:, :, :], ALU.mult).then_inc(ssm_ready, 1)
            if stop <= 11:
                return
            attention(ODD_JOBS, ATTN_E, oTo, 0)
            if stop <= 12:
                return
            gated_sum([(half, t) for half in range(2) for t in range(2)], 16, [3, 4, 5, 6])
            normed(3)
            modulate(3)
            if stop <= 14:
                return

            def R(i):
                return s5v[:, i, :].rearrange("p (t e) -> p t e", t=2)

            def wide(x):
                return x.unsqueeze(2).to_broadcast([P, 2, NE])

            top = s5v[:, R_T, :]
            dve.memset(acc[:, :, :], 0.0)
            dve.memset(pick[:, :, NE, :], 0.0)
            dve.wait_ge(logits, 1)
            step(dve.tensor_tensor(R(R_L), bank[2][:, 0:16].rearrange("p (t e) -> p t e", t=2),
                                   vec[:, V_RB:V_RB + 8].unsqueeze(1).to_broadcast([P, 2, NE]), ALU.add))
            step(dve.tensor_scalar(R(R_C), cst[:, C_IOTA:C_IOTA + 8].unsqueeze(1).to_broadcast([P, 2, NE]),
                                   -1.0, float(NE), ALU.mult, ALU.add))
            for k, (src, hot) in enumerate(((R_L, R_O1), (R_L2, R_O2))):
                step(dve.tensor_reduce(top[:, 8 + 2 * k:10 + 2 * k], R(src), AX, ALU.max))
                step(dve.tensor_tensor(R(R_EQ), R(src), wide(top[:, 8 + 2 * k:10 + 2 * k]), ALU.is_equal))
                step(dve.tensor_tensor(R(R_EQ), R(R_EQ), R(R_C), ALU.mult))
                step(dve.tensor_reduce(top[:, 12:14], R(R_EQ), AX, ALU.max))
                step(dve.tensor_tensor(R(hot), R(R_C), wide(top[:, 12:14]), ALU.is_equal))
                if k == 0:
                    step(dve.scalar_tensor_tensor(out=R(R_L2), in0=R(hot), scalar=-3.0e38, in1=R(R_L),
                                                  op0=ALU.mult, op1=ALU.add))
            step(dve.tensor_tensor(R(R_SEL), R(R_O1), R(R_O2), ALU.add))
            dve.tensor_tensor(top[:, 2:4], top[:, 10:12], top[:, 8:10], ALU.subtract).then_inc(top_gap, 1)
            dve.sem_inc(sel_ready, 1)
            dve.wait_ge(top_exp, 1)
            step(dve.tensor_scalar(top[:, 0:2], top[:, 4:6], 1.0, None, ALU.add))
            step(dve.reciprocal(top[:, 0:2], top[:, 0:2]))
            step(dve.tensor_tensor(top[:, 6:8], top[:, 0:2], top[:, 4:6], ALU.mult))
            dve.tensor_tensor(R(R_O1), R(R_O1), wide(top[:, 0:2]), ALU.mult)
            step(dve.tensor_tensor(R(R_O2), R(R_O2), wide(top[:, 6:8]), ALU.mult))
            step(dve.tensor_tensor(R(R_GATE), R(R_O1), R(R_O2), ALU.add))
            dve.wait_ge(ranks, 1)
            step(dve.tensor_copy(s5v[:, R_POS, :], bank[3][:, 0:16]))
            step(dve.tensor_scalar(s5v[:, R_POS2, :], bank[3][:, 0:16], -float(P), None, ALU.add))
            step(dve.tensor_reduce(top[:, 14:15], bank[3][:, 16:24], AX, ALU.max))
            dve.tensor_scalar(flag[:, :], top[:, 14:15], float(P), None, ALU.is_gt).then_inc(flag_ready, 1)

            def gathered(n, b):
                dve.wait_ge(e_gather, 2 * n + 2)
                for c in range(4, 8):
                    ins = dve.tensor_scalar(xe[:, b, c, :], bank[7][:, (c - 4) * P:(c - 3) * P], coef[:, 3, c, 0:1],
                                            mod[1][:, M_SH2 + c, 0:1], ALU.mult, ALU.add)
                ins.then_inc(xe_dve, 1)

            def experts(rnd):
                iota, rank = cst[:, C_IOTA:C_IOTA + P], (R_POS, R_POS2)[rnd]
                for e in range(NE):
                    for t in range(2):
                        c = 8 * t + e
                        dve.tensor_scalar(pick[:, t, e, :], iota, s5v[:, rank, c:c + 1], s5v[:, R_SEL, c:c + 1],
                                          ALU.is_equal, ALU.mult)
                        ins = dve.tensor_scalar(gpick[:, t, e, :], iota, s5v[:, rank, c:c + 1],
                                                s5v[:, R_GATE, c:c + 1], ALU.is_equal, ALU.mult)
                ins.then_inc(pick_ready, 1)
                for g in range(1, 4, 2):
                    dve.wait_ge(gpick_turned, 4 * rnd + g + 1)
                    dve.tensor_copy(gTall[:, 2 * g:2 * g + 2, :].rearrange("p e t -> p (e t)"),
                                    bank[2 + g][:, :]).then_inc(gta_dve, 1)
                gathered((NE + 1) * rnd, 0)
                with dve.Fori(0, NE // 2) as p:
                    for b in range(2):
                        n = 2 * p + b + NE * rnd
                        for m in range(W13_SLOTS):
                            dve.wait_ge(e_silu, W13_SLOTS * n + m + 1)
                            dve.tensor_tensor(he[:, m % 2, :], sile[:, m % 2, :], bank[m % 2][:, 256:512],
                                              ALU.mult).then_inc(e_gated, 1)
                        dve.wait_ge(e_down, W2_SLOTS * (n + 1))
                        dve.tensor_copy(ye[:, 512:1024], bank[5][:, :]).then_inc(y_dve, 1)
                        gathered(n + rnd + 1, 1 - b)
                        for k in range(4):
                            h, t = divmod(k, 2)
                            dve.wait_ge(e_scatter, 4 * n + k + 1)
                            x = acc[:, t, h * 512:(h + 1) * 512]
                            dve.tensor_tensor(x, x, bank[6 + k % 2][:, :], ALU.add).then_inc(e_added, 1)

            dve.sem_inc(e_gated, 2)
            experts(0)
            crowded = dve.value_load(flag[0:1, 0:1], min_val=0, max_val=1)
            with dve.If(crowded > 0):
                experts(1)
            for t in range(2):
                for h in range(2):
                    x = acc[:, t, h * 512:(h + 1) * 512]
                    step(dve.tensor_tensor(x, x, G2[:, h * 512:(h + 1) * 512], ALU.mult))
                    o = X[:, t, h * 512:(h + 1) * 512]
                    dve.tensor_tensor(o, o, x, ALU.add).then_inc(final_ready, 1)

        @block.gpsimd
        def _(pool):
            steps = [0]

            def step(ins):
                steps[0] += 1
                ins.then_inc(pool_step, 1)
                pool.wait_ge(pool_step, steps[0])

            def residual(half_tiles, r0):
                for k, (half, t) in enumerate(half_tiles):
                    r = r0 + k
                    pool.wait_ge(res_gated, r + 1)
                    x = X[:, t, half * 512:(half + 1) * 512]
                    pool.tensor_tensor(x, x, tmp[:, r % 2, :], ALU.add).then_inc(res_done, 1)

            def cmul(o, x, y, t):
                pool.tensor_tensor(t[0], x[0], y[0], ALU.mult)
                pool.tensor_tensor(t[1], x[1], y[1], ALU.mult)
                pool.tensor_tensor(t[2], x[0], y[1], ALU.mult)
                step(pool.tensor_tensor(t[3], x[1], y[0], ALU.mult))
                pool.tensor_tensor(o[0], t[0], t[1], ALU.subtract)
                step(pool.tensor_tensor(o[1], t[2], t[3], ALU.add))

            def V(i, n=1):
                return s5v[:, i:i + n, :].rearrange("p a u -> p (a u)")

            pool.wait_ge(vec_landed, 16)
            pool.wait_ge(s5_rden, 1)
            step(pool.tensor_scalar(V(3), vec[:, V_STEP:V_STEP + 16], -120.0, 88.0, ALU.max, ALU.min))
            step(pool.tensor_scalar(V(4), V(3), float(1 / np.log(2)), ROUND, ALU.mult, ALU.add))
            step(pool.tensor_scalar(V(4), V(4), -ROUND, None, ALU.add))
            for part in LN2_PARTS:
                step(pool.tensor_scalar(V(5), V(4), -part, None, ALU.mult))
                step(pool.tensor_tensor(V(3), V(3), V(5), ALU.add))
            step(pool.memset(V(0), 1.0))
            for n in range(9, 0, -1):
                step(pool.tensor_tensor(V(0), V(0), V(3), ALU.mult))
                step(pool.tensor_scalar(V(0), V(0), 1.0 / n, 1.0, ALU.mult, ALU.add))
            step(pool.tensor_scalar(V(4), V(4), 127.0, 0.0, ALU.add, ALU.max))
            step(pool.tensor_scalar(V(5).bitcast(I32), V(4), float(1 << 23), None, ALU.mult))
            step(pool.tensor_tensor(V(0), V(0), V(5), ALU.mult))
            W_, E_, T_, K_ = (V(3, 2), V(5, 2)), (V(7, 2), V(9, 2)), [V(11 + 2 * i, 2) for i in range(4)], V(19)
            pool.memset(V(3, 4), 0.0)
            step(pool.memset(V(7, 4), 0.0))
            step(pool.tensor_tensor(V(3), vec[:, V_ARE:V_ARE + 16], V(0), ALU.mult))
            step(pool.tensor_scalar(V(3), V(3), -87.0, 87.0, ALU.max, ALU.min))
            step(pool.tensor_tensor(V(6), vec[:, V_AIM:V_AIM + 16], V(0), ALU.mult))
            step(pool.tensor_scalar(K_, V(6), 1.0 / (2 * np.pi), ROUND, ALU.mult, ALU.add))
            step(pool.tensor_scalar(K_, K_, -ROUND, None, ALU.add))
            for part in TURN_PARTS:
                step(pool.tensor_scalar(V(20), K_, -part, None, ALU.mult))
                step(pool.tensor_tensor(V(6), V(6), V(20), ALU.add))
            step(pool.tensor_scalar(V(3, 4), V(3, 4), 1.0 / 256, None, ALU.mult))
            step(pool.tensor_scalar(E_[0], E_[0], 1.0, None, ALU.add))
            for n in range(8, 1, -1):
                cmul(E_, E_, W_, T_)
                step(pool.tensor_scalar(V(7, 4), V(7, 4), 1.0 / n, None, ALU.mult))
                step(pool.tensor_scalar(E_[0], E_[0], 1.0, None, ALU.add))
            cmul(E_, E_, W_, T_)
            for _ in range(8):
                step(pool.tensor_scalar(W_[0], E_[0], 2.0, None, ALU.add))
                cmul(E_, E_, (W_[0], E_[1]), T_)
            step(pool.tensor_tensor(V(3), V(7), V(8), ALU.mult))
            step(pool.tensor_tensor(V(3), V(3), V(7), ALU.add))
            step(pool.tensor_tensor(V(3), V(3), V(8), ALU.add))
            step(pool.tensor_tensor(V(4), V(7), V(10), ALU.mult))
            step(pool.tensor_tensor(V(4), V(4), V(10), ALU.add))
            are, aim = vec[:, V_ARE:V_ARE + 16], vec[:, V_AIM:V_AIM + 16]
            step(pool.tensor_scalar(V(11), aim, -1.0, None, ALU.mult))
            cmul((V(5), V(6)), (V(3), V(4)), (are, V(11)), [V(12), V(13), V(14), V(15)])
            step(pool.tensor_tensor(V(5), V(5), V(1), ALU.mult))
            step(pool.tensor_tensor(V(6), V(6), V(1), ALU.mult))
            step(pool.tensor_scalar(V(S_R), V(7), 1.0, None, ALU.add))
            step(pool.tensor_scalar(V(S_PW), V(8), 1.0, None, ALU.add))
            step(pool.tensor_scalar(V(S_PW + 1), V(10), 0.0, None, ALU.add))
            if stop <= 1:
                return
            for j in range(8):
                n, t = divmod(j, 4)
                pool.wait_ge(in_normed, j + 1)
                hg = H_EQ if n == 0 else H_EK
                v = hn[:, 1 + n, t, :].rearrange("p (h d) -> p h d", d=HD)
                pool.tensor_tensor(v, v, vec[:, V_HEAD + hg * HD:V_HEAD + (hg + 1) * HD].unsqueeze(1)
                                   .to_broadcast([P, 8, HD]), ALU.mult).then_inc(head_ready, 1)
            if stop <= 3:
                return

            def load_bias(h):
                for t in range(2):
                    for q in range(2):
                        row = 2 * t + q
                        src = bass.AP(a["rpb"].tensor, (h * NA_DR + 7 - row) * RPB_PAD,
                                      [[1, GRID_W], [RPB_PAD, ROWS], [1, GRID_W]])
                        pool.dma_start(bias_raw[64 * q:64 * q + 64, h % 2, t * SEQ:(t + 1) * SEQ]
                                       .rearrange("p (r c) -> p r c", r=ROWS), src).then_inc(bias_landed[h % 2], 16)

            load_bias(0)
            for h in range(NA_HEADS):
                if h + 1 < NA_HEADS:
                    if h >= 1:
                        pool.wait_ge(bias_ready, h)
                    load_bias(h + 1)
                pool.wait_ge(bias_landed[h % 2], 64 * (h // 2 + 1))
                if h >= 2:
                    pool.wait_ge(bias_used, 2 * (h - 1))
                b = bias[:, h % 2, :].rearrange("p (r c) -> p r c", c=GRID_W)
                raw = bias_raw[:, h % 2, :].rearrange("p (r c) -> p r c", c=GRID_W)
                pool.tensor_tensor(b, raw[:, :, ::-1], cst[:, C_MASK:C_MASK + GRID_W].unsqueeze(1)
                                   .to_broadcast([P, 2 * ROWS, GRID_W]), ALU.add).then_inc(bias_ready, 1)
            if stop <= 4:
                return
            halves4 = [(half, t) for half in range(2) for t in range(4)]
            residual(halves4, 0)
            if stop <= 6:
                return
            residual(halves4, 8)
            if stop <= 8:
                return

            pool.wait_ge(s5_raw, 32)
            cf = [V(5 + i).unsqueeze(2).to_broadcast([P, UNITS, 32]) for i in range(2)]
            for i, (x, y, op) in enumerate(((0, 1, ALU.subtract), (1, 0, ALU.add))):
                pool.tensor_tensor(b_bar[i], b_raw[x], cf[0], ALU.mult)
                step(pool.tensor_tensor(b_tmp, b_raw[y], cf[1], ALU.mult))
                ins = pool.tensor_tensor(b_bar[i], b_bar[i], b_tmp, op)
                if i == 0:
                    step(ins)
            ins.then_inc(s5_bbar, 1)

            for i, (n, t) in enumerate(IN_JOBS[:8]):
                heads = (8, 4, 3)[n]
                pool.wait_ge(in_normed, 8 + i + 1)
                v = (kn[:, t, :, 0, :] if n == 2 else
                     qn[:, t, 512 * n:512 * n + heads * HD].rearrange("p (h d) -> p h d", d=HD))
                hg = H_OK if n == 2 else H_OQ

                def over_heads(x, w=HD):
                    return x.unsqueeze(1).to_broadcast([P, heads, w])

                ins = pool.tensor_tensor(v, v, over_heads(vec[:, V_HEAD + hg * HD:V_HEAD + (hg + 1) * HD]), ALU.mult)
                if t < LAT_TILES:
                    step(ins)
                    cos = cst[:, C_COS + t * HD:C_COS + (t + 1) * HD]
                    sin = cst[:, C_SIN + t * HD:C_SIN + (t + 1) * HD]
                    r = rope_t[:, 0:heads * HD].rearrange("p (h d) -> p h d", d=HD)
                    pool.tensor_tensor(r[:, :, 0::2], v[:, :, 1::2], over_heads(sin[:, 0::2], HD // 2), ALU.mult)
                    step(pool.tensor_tensor(r[:, :, 1::2], v[:, :, 0::2], over_heads(sin[:, 1::2], HD // 2), ALU.mult))
                    step(pool.tensor_tensor(v, v, over_heads(cos), ALU.mult))
                    ins = pool.tensor_tensor(v, v, r, ALU.add)
                if n == 2:
                    step(ins)
                    ins = pool.tensor_copy(kn[:, t, :, 1, :], kn[:, t, :, 0, :])
                ins.then_inc(head_ready, 1)
            if stop <= 10:
                return

            pool.wait_ge(s5_turned, 2)

            def powers(tab, m, n, row):
                pw = [V(row + i).unsqueeze(2).to_broadcast([P, UNITS, m]) for i in range(2)]
                t = [x[:, 0:UNITS * m].rearrange("p (u n) -> p u n", u=UNITS) for x in p4]
                cmul([x[:, :, m:2 * m] for x in tab], [x[:, :, 0:m] for x in tab], pw, t)

            for tab in (lo, hi):
                for i in range(2):
                    step(pool.memset(tab[i][:, :, 0:1], 1.0 - i))
            for k in range(9):
                row = S_PW
                tab, m = (lo, 1 << k) if k < 4 else (hi, 1 << (k - 4))
                powers(tab, m, 2 * m, row)
                if k < 8:
                    cmul((V(S_PW), V(S_PW + 1)), (V(S_PW), V(S_PW + 1)), (V(S_PW), V(S_PW + 1)),
                         [V(11), V(12), V(13), V(14)])
            for k in range(UNITS):
                j, d = divmod(k, 2)
                u = PAIRS * d + j
                h = [x[:, u, :].unsqueeze(2).to_broadcast([P, 32, 16]) for x in hi]
                l = [x[:, u, :].unsqueeze(1).to_broadcast([P, 32, 16]) for x in lo]
                o = [turn[:, k % 2, i, :].rearrange("p (a b) -> p a b", a=32) for i in range(2)]
                t = [x.rearrange("p (a b) -> p a b", a=32) for x in pt]
                if k >= 2:
                    pool.wait_ge(s5_s, k - 1)
                pool.tensor_tensor(t[0], h[0], l[0], ALU.mult)
                step(pool.tensor_tensor(t[1], h[1], l[1], ALU.mult))
                step(pool.tensor_tensor(o[0], t[0], t[1], ALU.subtract))
                pool.tensor_tensor(t[0], h[0], l[1], ALU.mult)
                step(pool.tensor_tensor(t[1], h[1], l[0], ALU.mult))
                pool.tensor_tensor(o[1], t[0], t[1], ALU.add).then_inc(s5_table, 1)
                pool.wait_ge(s5_table, k + 1)
            if stop <= 12:
                return
            residual([(half, t) for half in range(2) for t in range(2)], 16)
            if stop <= 14:
                return

            def experts(rnd):
                pool.wait_ge(gta_act, 2 * (rnd + 1))
                pool.wait_ge(gta_dve, 2 * (rnd + 1))
                with pool.Fori(0, NE // 2) as p:
                    for b in range(2):
                        n = 2 * p + b + NE * rnd
                        pool.wait_ge(e_gather, 2 * (n + rnd) + 2)
                        pool.tensor_copy(gTe[:, b, :], gTall[:, bass.ds(2 * p + b, 1), :]
                                         .rearrange("p o t -> p (o t)")).then_inc(gte_ready, 1)

            experts(0)
            pool.wait_ge(flag_ready, 1)
            crowded = pool.value_load(flag[0:1, 0:1], min_val=0, max_val=1)
            with pool.If(crowded > 0):
                experts(1)


_OUTS = [((1, SEQ, D), "float32")]


def host_layout(inp):
    f = {k: np.ascontiguousarray(np.asarray(v)) for k, v in inp.items()}
    v = np.zeros((P, V_ALL), np.float32)

    def cols(x):
        return x.reshape(-1, P).T

    v[:, V_COND:V_COND + 16] = np.stack([cols(f["c"][0]), cols(f["c_ctx"])], 2).reshape(P, 16)
    for q, n in enumerate(("ev_norm_mix", "ev_norm_ffn", "od_norm_mix", "od_norm_ffn")):
        v[:, V_NORM + 8 * q:V_NORM + 8 * q + 8] = cols(f[n][0])
    for q, n in enumerate(("ev_mod_b", "od_mod_b")):
        v[:, V_MODB + 48 * q:V_MODB + 48 * q + 48] = cols(f[n][0])

    def states(x):
        return x.reshape(2, PAIRS, 2 * S5_STATE).transpose(2, 0, 1).reshape(P, UNITS)

    v[:, V_ARE:V_ARE + 16] = states(f["od_s5_a_re"][0])
    v[:, V_AIM:V_AIM + 16] = states(f["od_s5_a_im"][0])
    v[:, V_STEP:V_STEP + 16] = states(np.repeat(f["od_s5_log_step"][0][:, :, None], S5_STATE, 2))
    v[:, V_D:V_D + 2] = cols(f["od_s5_d"][0])
    v[:, V_GLUB:V_GLUB + 2] = cols(f["od_s5_glu_b"][0])
    for q, n in enumerate(("ev_q_gain", "ev_k_gain", "od_q_gain", "od_k_gain")):
        v[:, V_HEAD + HD * q:V_HEAD + HD * (q + 1)] = f[n][0][None, :]
    v[:, V_RW:V_RW + 64] = f["od_router_w"][0].reshape(DC, P, NE).transpose(1, 0, 2).reshape(P, 64)
    v[:, V_RB:V_RB + 8] = f["od_router_b"][0][None, :]
    rpb = np.zeros((NA_HEADS, NA_DR, RPB_PAD), np.float32)
    rpb[:, :, 63 - (NA_KW - 1):63 + NA_KW] = f["ev_rpb"][0][:, :, ::-1]
    bb = np.zeros((2, 2, S5_STATE, UNITS, 2, S5_DIM), np.float32)
    cc = np.zeros((2, 2, S5_STATE, UNITS, 2, S5_DIM), np.float32)
    for part, s in enumerate(("re", "im")):
        for g in range(2):
            bb[part, g, :, :, g, :] = (f[f"od_s5_b_{s}"][0].reshape(2, PAIRS, 2, S5_STATE, S5_DIM)[:, :, g]
                                       .transpose(2, 0, 1, 3).reshape(S5_STATE, UNITS, S5_DIM))
            cc[part, g, :, :, g, :] = (f[f"od_s5_c_{s}"][0].reshape(2, PAIRS, 2, S5_DIM, S5_STATE)[:, :, g]
                                       .transpose(3, 0, 1, 2).reshape(S5_STATE, UNITS, S5_DIM))
    arrays = {"vec": v, "cst": constants(), "dft": dft_constants(), "rpb": rpb,
              "s5b": bb.reshape(2, P, UNITS * 32), "s5c": cc.reshape(2, P, UNITS * 32)}
    for n in ("x", "ctx", "ev_mod_w", "ev_w_in", "ev_w_out", "ev_ffn_w1", "ev_ffn_w3", "ev_ffn_w2", "od_mod_w",
              "od_w_in", "od_s5_glu_w", "od_w_out", "od_router_w", "od_exp_w1", "od_exp_w3", "od_exp_w2"):
        arrays[n] = f[n]
    return arrays


def kernel(**inputs):
    import concourse.bacc as bacc
    from concourse.bass_utils import run_bass_kernel_spmd

    nc = bacc.Bacc("TRN2", target_bir_lowering=False, num_devices=1)
    arrays = host_layout(inputs)
    a = {n: nc.dram_tensor(f"in_{n}", x.shape, mybir.dt.from_np(x.dtype), kind="ExternalInput").ap()
         for n, x in arrays.items()}
    out = nc.dram_tensor("out_0", _OUTS[0][0], F32, kind="ExternalOutput").ap()
    build(nc, a, out)
    r = run_bass_kernel_spmd(nc, [{f"in_{n}": x for n, x in arrays.items()}], core_ids=[0])
    return r.results[0]["out_0"]
```

```python
from contextlib import ExitStack

import numpy as np

import concourse.bass as bass
from concourse import mybir

F32 = mybir.dt.float32
F32R = mybir.dt.float32r
I32 = mybir.dt.int32
ALU = mybir.AluOpType
ACT = mybir.ActivationFunctionType
AX = mybir.AxisListType.X

P = 128
D = 1024
DC = D // P
SEQ = CTX = 256
GRID_W = 64
LAT_TILES, TILES = SEQ // P, (SEQ + CTX) // P
TOK = SEQ + CTX
HD = 64
NA_HEADS, NA_KW, NA_DR = 8, 16, 15
ROWS = SEQ // GRID_W
QH, KVH = 12, 3
S5_GROUPS, S5_DIM, S5_STATE = 16, 16, 64
PAIRS = S5_GROUPS // 2
UNITS = 2 * PAIRS
FF = 2816
FC = FF // P
NE, FE = 8, 3584
EC = FE // P
EPS = 1e-6
RPB_PAD = 127

RING, HALVES, HALF = 3, 6, 2048
FG = [6, 6, 6, 4]
UP_SLOTS, DOWN_SLOTS = FC // 2, 2 * len(FG)
S_MOD, S_IN_E, S_OUT_E, S_FFN = [0, 16], 12, 28, 30
S_IN_O = S_FFN + UP_SLOTS + DOWN_SLOTS
S_OUT_O = S_IN_O + 4
S_MOE = S_OUT_O + 2
W13_SLOTS, W2_SLOTS = EC // 2, EC // 4
GATHER_AT = 8
E_UNITS = 2 * (W13_SLOTS + W2_SLOTS)
AHEAD = 3
F_UNITS = 2 * (UP_SLOTS + DOWN_SLOTS)
PASSES = ((0, 0), (0, 1), (1, 0))
RES_FFN = 8 * len(FG)

C_ID, C_REV, C_TRI, C_ONE, C_IOTA, C_MASK, C_COS, C_SIN = 0, 128, 256, 384, 512, 640, 704, 832
C_ALL = 960
V_COND, V_NORM, V_MODB, V_ARE, V_AIM, V_STEP, V_D, V_GLUB = 0, 16, 48, 144, 160, 176, 192, 194
V_HEAD, V_RB, V_RW, V_ALL = 196, 452, 460, 524
H_EQ, H_EK, H_OQ, H_OK = range(4)
M_SH1, M_SC1, M_G1, M_SH2, M_SC2, M_G2 = range(0, 48, 8)


S_R, S_PW = 21, 22
ROUND = 12582912.0
LN2_PARTS = (0.693359375, float(np.log(2) - 0.693359375))
TURN_PARTS = (6.28125, 0.0019340515136718750, float(2 * np.pi - 6.28125 - 0.0019340515136718750))


def constants():
    c = np.zeros((P, C_ALL), np.float32)
    i = np.arange(P)
    c[i, C_ID + i] = 1.0
    c[i, C_REV + P - 1 - i] = 1.0
    c[:, C_TRI:C_TRI + P] = i[:, None] < i[None, :]
    c[:, C_ONE:C_ONE + P] = 1.0
    c[:, C_IOTA:C_IOTA + P] = i[None, :]
    q, k = (i % GRID_W)[:, None], np.arange(GRID_W)[None, :]
    start = np.clip(q - NA_KW // 2, 0, GRID_W - NA_KW)
    c[:, C_MASK:C_MASK + GRID_W] = np.where((k >= start) & (k < start + NA_KW), 0.0, -1e30)
    freq = 10000.0 ** (-np.arange(HD // 4, dtype=np.float32) / np.float32(HD // 4))
    for t in range(LAT_TILES):
        tok = t * P + i
        ang = np.concatenate([(tok // GRID_W)[:, None].astype(np.float32) * freq,
                              (tok % GRID_W)[:, None].astype(np.float32) * freq], 1).astype(np.float32)
        cos, sin = np.cos(ang), np.sin(ang)
        c[:, C_COS + t * HD:C_COS + (t + 1) * HD] = np.repeat(cos, 2, 1)
        c[:, C_SIN + t * HD:C_SIN + (t + 1) * HD] = np.stack([-sin, sin], 2).reshape(P, HD)
    return c


def dft_constants():
    n = np.arange(SEQ)
    ang = 2 * np.pi * ((n[:, None] * n[None, :]) % SEQ) / SEQ
    tok = np.concatenate([np.cos(ang), np.sin(ang)], 1).reshape(2, P, 2 * SEQ).transpose(1, 0, 2)
    n = np.arange(P)
    ang = 2 * np.pi * ((n[:, None] * n[None, :]) % P) / P
    ch = np.concatenate([np.cos(ang), -np.sin(ang)], 1) / np.sqrt(SEQ * P)
    return np.concatenate([tok.reshape(P, 4 * SEQ), ch], 1).astype(np.float32)


def build(nc, a, out):
    ctx = ExitStack()
    with ctx:
        def sb(name, shape, dt=F32):
            return ctx.enter_context(nc.sbuf_tensor(name, shape, dt))

        def sem(name):
            return ctx.enter_context(nc.semaphore(name))

        bank = [ctx.enter_context(nc.psum_tensor(f"bank{i}", [P, 512], F32)) for i in range(8)]
        with nc.sbuf_tensor("ring", [P, HALVES, HALF], F32) as ring:
            pass
        with nc.sbuf_tensor("rest", [P, HALVES, HALF], F32R) as rest:
            pass
        sb("held_ring", [P, HALVES, HALF])
        with nc.sbuf_tensor("rows", [P, 6 * D], F32) as rows:
            pass
        WR = sb("WR", [P, HALVES, HALF], F32R)
        X = sb("X", [P, TILES, D])
        with ExitStack() as mixing:
            def mix(name, shape, dt=F32):
                return mixing.enter_context(nc.sbuf_tensor(name, shape, dt))

            S = mix("S", [P, 6656])
            HT = mix("HT", [P, 4096])
            B = mix("B", [P, FC * TOK])
        with ExitStack() as dense:
            def ffn(name, shape, dt=F32):
                return dense.enter_context(nc.sbuf_tensor(name, shape, dt))

            GF = ffn("GF", [P, 2, D])
            tmpf = ffn("tmpf", [P, 2, 512])
            hf = ffn("hf", [P, 4, TOK])
            hTr = ffn("hTr", [P, 2, DC, TOK], F32R)
            with nc.sbuf_tensor("gTr", [P, 2, max(FG), TOK], F32R) as gTr:
                pass
            xnf = ffn("xnf", [P, TILES, D])
        with ExitStack() as moe:
            def exp(name, shape, dt=F32):
                return moe.enter_context(nc.sbuf_tensor(name, shape, dt))

            heTr = exp("heTr", [P, 2, EC, P], F32R)
            xer = exp("xer", [P, 2, DC, P], F32R)
            he = exp("he", [P, 2, 256])
            sile = exp("sile", [P, 2, 256])
            gTe = exp("gTe", [P, SEQ])
        sb("held", [P, 6656 + 4096 + FC * TOK])
        cst = sb("cst", [P, C_ALL])
        vec = sb("vec", [P, V_ALL])
        silc = sb("silc", [P, DC, 2])
        mod = [sb(f"mod{i}", [P, 48, 2]) for i in range(2)]
        coef = sb("coef", [P, 4, DC, 2])
        ss = sb("ss", [P, TILES])
        rstd = sb("rstd", [P, TILES])
        hss = sb("hss", [P, QH])
        nmax = sb("nmax", [P, 4])
        rsum = sb("rsum", [P, 4])
        rinv = sb("rinv", [P, 4])

        ident = cst[:, C_ID:C_ID + P]
        rev = cst[:, C_REV:C_REV + P]
        hT = HT[:, :].rearrange("p (c t) -> p c t", c=DC)
        xn = B[:, 0:TILES * D].rearrange("p (t d) -> p t d", t=TILES)
        hn = B[:, 0:4 * TOK * 4].rearrange("p (n t c) -> p n t c", n=4, t=TILES)
        oT = B[:, 2048:2048 + DC * TOK].rearrange("p (c t) -> p c t", c=DC)
        G = S[:, 0:2 * D].rearrange("p (s d) -> p s d", s=2)
        mrow = S[:, 4096:5120].rearrange("p (b n) -> p b n", b=2)
        sq = S[:, 2048:3072].rearrange("p (b n) -> p b n", b=2)
        tmp = S[:, 2048:3072].rearrange("p (b n) -> p b n", b=2)
        sil, gf = hf[:, 0:2, :], hf[:, 2:4, :]
        T1 = S[:, 4096:5120].rearrange("p (b n) -> p b n", b=2)
        dft = S[:, 5120:6400]
        bias = S[:, 0:1024].rearrange("p (b n) -> p b n", b=2)
        bias_raw = B[:, 8192:9216].rearrange("p (b n) -> p b n", b=2)
        prob = S[:, 1024:2560].rearrange("p (b n) -> p b n", b=3)
        pT = S[:, 2560:4608].rearrange("p (b k q) -> p b k q", b=2, k=4)

        s5v = sb("s5v", [P, 32, UNITS])
        flag = sb("flag", [P, 1], I32)
        qn = B[:, 0:1536].rearrange("p (t c) -> p t c", t=2)
        kn = B[:, 1536:3072].rearrange("p (t h b d) -> p t h b d", t=TILES, h=KVH, b=2)
        vn = B[:, 3072:3840].rearrange("p (t c) -> p t c", t=TILES)
        un = B[:, 3840:4864].rearrange("p (t c) -> p t c", t=TILES)
        oTo = B[:, 4864:6912].rearrange("p (c t) -> p c t", c=DC)
        uT = [B[:, 6912 + 1024 * d:7936 + 1024 * d].rearrange("p (c t) -> p c t", c=2) for d in range(2)]
        BT = [B[:, 8960 + 512 * i:9472 + 512 * i] for i in range(2)]
        C5 = [B[:, 9984 + 512 * i:10496 + 512 * i].rearrange("p (u n) -> p u n", u=UNITS) for i in range(2)]
        gluw = B[:, 1536:2048].rearrange("p (k n) -> p k n", k=2)
        qTo = HT[:, 0:1536].rearrange("p (c t) -> p c t", c=6)
        kTo = HT[:, 1536:3072].rearrange("p (c t) -> p c t", c=KVH)
        s_out = X[:, 2:4, :].rearrange("p b (i t) -> p b i t", i=4)
        C5neg = HT[:, 3072:3584].rearrange("p (u n) -> p u n", u=UNITS)
        sqo = S[:, 1536:2560].rearrange("p (b n) -> p b n", b=2)
        rope_t = S[:, 2560:3072]
        b_raw = [S[:, 5632 + 512 * i:6144 + 512 * i].rearrange("p (u n) -> p u n", u=UNITS) for i in range(2)]
        b_bar = [S[:, 4608 + 512 * i:5120 + 512 * i].rearrange("p (u n) -> p u n", u=UNITS) for i in range(2)]
        lo = [S[:, 1024 + 256 * i:1280 + 256 * i].rearrange("p (u n) -> p u n", u=UNITS) for i in range(2)]
        hi = [S[:, 512 * i:512 + 512 * i].rearrange("p (u n) -> p u n", u=UNITS) for i in range(2)]
        turn = S[:, 1536:3584].rearrange("p (b i t) -> p b i t", b=2, i=2)
        pt = [S[:, 3584 + 512 * i:4096 + 512 * i] for i in range(2)]
        z = [S[:, 4608 + 512 * i:5120 + 512 * i] for i in range(2)]
        vt = [S[:, 5632 + 512 * i:6144 + 512 * i] for i in range(2)]
        b_tmp = S[:, 3072:3584].rearrange("p (u n) -> p u n", u=UNITS)
        p4 = [S[:, 3584 + 256 * i:3840 + 256 * i] for i in range(4)]
        y5 = S[:, 5632:6144].rearrange("p (c t) -> p c t", c=2)
        y5s = S[:, 6144:6656].rearrange("p (c t) -> p c t", c=2)

        pick = B[:, 2048:4352].rearrange("p (t e s) -> p t e s", t=2, e=NE + 1)
        gTall = B[:, 4352:6400].rearrange("p (e t) -> p e t", e=NE)
        gpick = B[:, 6400:8448].rearrange("p (t e s) -> p t e s", t=2, e=NE)
        xf = B[:, 6400:7424].rearrange("p (c s) -> p c s", c=DC)
        ye = B[:, 8448:9472]
        G2 = B[:, 9472:10496]
        acc = X[:, 2:4, :]

        half_landed = [sem(f"half{i}_landed") for i in range(HALVES)]
        split_hi, split_lo, unit_done = sem("split_hi"), sem("split_lo"), sem("unit_done")
        vec_landed, cst_landed, x_landed, dft_landed = (
            sem("vec_landed"), sem("cst_landed"), sem("x_landed"), sem("dft_landed"))
        dve_step, act_step, pool_step = sem("dve_step"), sem("act_step"), sem("pool_step")
        cond_ready, mod_psum, mod_row, mod_turned, mod_ready = (
            sem("cond_ready"), sem("mod_psum"), sem("mod_row"), sem("mod_turned"), sem("mod_ready"))
        coef_ready, square_sum, xn_ready, xn_turned, ht_act, ht_dve = (
            sem("coef_ready"), sem("square_sum"), sem("xn_ready"), sem("xn_turned"), sem("ht_act"), sem("ht_dve"))
        in_psum, in_copied, in_squared, in_summed, in_normed, head_ready = (
            sem("in_psum"), sem("in_copied"), sem("in_squared"), sem("in_summed"), sem("in_normed"), sem("head_ready"))
        qk_turned, qk_act, qk_dve = sem("qk_turned"), sem("qk_act"), sem("qk_dve")
        four_a, four_t, four_b, four_o = sem("four_a"), sem("four_t"), sem("four_b"), sem("four_o")
        bias_landed = [sem("bias0_landed"), sem("bias1_landed")]
        bias_ready, bias_used = sem("bias_ready"), sem("bias_used")
        scores, row_max, exp_done, prob_ready, prob_turned, pt_ready, o_psum, o_ready = (
            sem("scores"), sem("row_max"), sem("exp_done"), sem("prob_ready"), sem("prob_turned"),
            sem("pt_ready"), sem("o_psum"), sem("o_ready"))
        gate_psum, gate_ready = sem("gate_psum"), sem("gate_ready")
        res_psum, res_gated, res_done = sem("res_psum"), sem("res_gated"), sem("res_done")
        up_silu, g_full, g_hi, g_lo = sem("up_silu"), sem("g_full"), sem("g_hi"), sem("g_lo")
        ht_hi, ht_lo = sem("ht_hi"), sem("ht_lo")
        mean_ready, root_ready = sem("mean_ready"), sem("root_ready")
        s5_rden, s5_raw, s5_c, s5_bbar, s5_turned, s5_bt_act, s5_bt_dve = (
            sem("s5_rden"), sem("s5_raw"), sem("s5_c"), sem("s5_bbar"), sem("s5_turned"),
            sem("s5_bt_act"), sem("s5_bt_dve"))
        s5_table, s5_bu, s5_bu_used, s5_s, s5_y = (
            sem("s5_table"), sem("s5_bu"), sem("s5_bu_used"), sem("s5_s"), sem("s5_y"))
        y5_ready, y5_gelu, glu_landed, glu_psum, glu_sig, ssm_ready = (
            sem("y5_ready"), sem("y5_gelu"), sem("glu_landed"), sem("glu_psum"), sem("glu_sig"), sem("ssm_ready"))
        logits, top_gap, top_exp, sel_ready, ranks, flag_ready = (
            sem("logits"), sem("top_gap"), sem("top_exp"), sem("sel_ready"), sem("ranks"), sem("flag_ready"))
        pick_ready, gpick_turned, gta_act, gta_dve = (
            sem("pick_ready"), sem("gpick_turned"), sem("gta_act"), sem("gta_dve"))
        e_gather, xf_act, xf_dve, xe_hi, xe_lo, e_silu, e_gated, e_turned, heT_hi, heT_lo = (
            sem("e_gather"), sem("xf_act"), sem("xf_dve"), sem("xe_hi"), sem("xe_lo"), sem("e_silu"),
            sem("e_gated"), sem("e_turned"), sem("heT_hi"), sem("heT_lo"))
        y_act, y_dve, e_scatter, e_added, gte_ready = (
            sem("y_act"), sem("y_dve"), sem("e_scatter"), sem("e_added"), sem("gte_ready"))
        final_ready, halves_reused = sem("final_ready"), sem("halves_reused")
        out_done = sem("out_done")

        block = ctx.enter_context(nc.Block())

        def part(i, h, n=HALF):
            return (WR if i == 0 else rest)[:, h % HALVES, 0:n]

        def slot(i):
            return ring[:, 2 * (i % RING):2 * (i % RING) + 2, :].rearrange("p h n -> p (h n)")

        def wait_slot(eng, i):
            for h in (2 * i, 2 * i + 1):
                eng.wait_ge(half_landed[h % HALVES], 32 * (h // HALVES + 1))

        F_ORDER, F_SLOTS = [], []
        for q, ks in enumerate(FG):
            for n in range(sum(FG[:q]) // 2, sum(FG[:q + 1]) // 2):
                F_SLOTS.append(("up", n))
                F_ORDER += [("up", n, m) for m in range(2)]
            for d in range(2):
                F_SLOTS.append(("down", q, d))
                F_ORDER += [("down", q, d, kh) for kh in range(2)]

        def read(i):
            if i < S_IN_E:
                return mod_psum, i + 1
            if i < S_MOD[1]:
                return in_psum, 4 * (i - S_IN_E + 1)
            if i < S_OUT_E:
                return mod_psum, 12 + i - S_MOD[1] + 1
            if i < S_FFN:
                return res_psum, 4 * (i - S_OUT_E + 1)
            if i < S_IN_O:
                return unit_done, 2 * (i - S_FFN + 1)
            if i < S_OUT_O:
                return in_psum, 16 + [2, 4, 8, 12][i - S_IN_O]
            return res_psum, 8 + 2 * (i - S_OUT_O + 1)

        IN_COLS = [(0, 512), (512, 256), (768, 384), (1152, 256)]
        IN_JOBS = [(n, t) for n in range(4) for t in range(LAT_TILES if n < 2 else TILES)]
        ATTN_E = 4 * NA_HEADS

        def unit_width(g):
            what = F_ORDER[g]
            return HALF if what[0] == "up" else FG[what[1]] // 2 * 512

        MOD_FILL = []
        for n in range(12):
            cuts = (0, 4, 8) if n < 4 else (0, 3, 6, 8)
            MOD_FILL += [(n, range(x, y)) for x, y in zip(cuts, cuts[1:])]

        NORMS = [(0, M_SH1, M_SC1, 4, 0), (0, M_SH2, M_SC2, 4, 8),
                 (1, M_SH1, M_SC1, 4, 8 + RES_FFN), (1, M_SH2, M_SC2, 2, 12 + RES_FFN)]
        def XN(q):
            return xnf if q == 1 else xn

        GATES = [(0, M_G1, 2), (0, M_G2, 2), (1, M_G1, 1), (1, M_G2, 1)]

        qT, kT = hT[:, 0:4], hT[:, 4:8]

        def even_jobs():
            jobs = []
            for h in range(NA_HEADS):
                rows = slice(64 * (h % 2), 64 * (h % 2) + HD)
                for t in range(2):
                    jobs.append((qT[rows, h // 2, t * P:(t + 1) * P], kT[rows, h // 2, :], TOK,
                                 [hn[:, 3, k, h * HD:(h + 1) * HD] for k in range(4)], h % 2, h, 0))
            for h in range(NA_HEADS):
                rows = slice(64 * (h % 2), 64 * (h % 2) + HD)
                for t in range(2, 4):
                    jobs.append((qT[rows, h // 2, t * P:(t + 1) * P], kT[rows, h // 2, SEQ:], CTX,
                                 [hn[:, 3, 2 + k, h * HD:(h + 1) * HD] for k in range(2)], h % 2, h, 1))
            return jobs

        EVEN_JOBS = even_jobs()
        ODD_JOBS = [(qTo[64 * (h % 2):64 * (h % 2) + HD, h // 2, t * P:(t + 1) * P],
                     kTo[64 * (h % 2):64 * (h % 2) + HD, h // 4, :], TOK,
                     [vn[:, k, (h // 4) * HD:(h // 4 + 1) * HD] for k in range(4)], h % 2, h, 0)
                    for h in range(QH) for t in range(2)]
        (R_L, R_EQ, R_L2, R_C, R_O1, R_O2, R_SEL, R_GATE, R_POS, R_POS2, R_T) = range(11)

        @block.sync
        def _(sp):
            def load(i, parts):
                if i >= RING:
                    sp.wait_ge(*read(i - RING))
                for k, (dst, src) in enumerate(parts):
                    sp.dma_start(dst, src).then_inc(half_landed[(2 * i + k // 2) % HALVES], 16)

            def columns(i, w, lo, n):
                dst = slot(i)[:, 0:DC * n].rearrange("p (k n) -> p k n", k=DC)
                src = w.rearrange("(k p) n -> p k n", p=P)[:, :, lo:lo + n]
                load(i, [(dst[:, k:k + 2], src[:, k:k + 2]) for k in range(0, DC, 2)])

            def up_slot(i, n):
                dst = slot(i).rearrange("p (m k n) -> p m k n", m=2, k=DC)
                src = [a[w][0].rearrange("(k p) n -> p k n", p=P) for w in ("ev_ffn_w1", "ev_ffn_w3")]
                load(i, [(dst[:, m, k:k + 4], src[m][:, k:k + 4, 256 * n:256 * n + 256])
                         for m in range(2) for k in (0, 4)])

            def down_slot(i, q, d):
                k0, ks = sum(FG[:q]), FG[q] // 2
                dst = ring[:, 2 * (i % RING):2 * (i % RING) + 2, 0:ks * 512].rearrange("p h (k n) -> p h k n", k=ks)
                src = a["ev_ffn_w2"][0].rearrange("(k p) n -> p k n", p=P)[:, :, 512 * d:512 * d + 512]
                load(i, [(dst[:, h, k:e], src[:, k0 + ks * h + k:k0 + ks * h + e])
                         for h in range(2) for k, e in ((0, 1), (1, ks))])

            for n in range(12):
                columns(S_MOD[0] + n, a["ev_mod_w"][0], 512 * n, 512)
            for n in range(4):
                columns(S_IN_E + n, a["ev_w_in"][0], 512 * n, 512)
            for n in range(12):
                columns(S_MOD[1] + n, a["od_mod_w"][0], 512 * n, 512)
            for n in range(2):
                columns(S_OUT_E + n, a["ev_w_out"][0], 512 * n, 512)
            for j, what in enumerate(F_SLOTS):
                (up_slot if what[0] == "up" else down_slot)(S_FFN + j, *what[1:])
            for n, (lo_, w_) in enumerate(IN_COLS):
                columns(S_IN_O + n, a["od_w_in"][0], lo_, w_)
            for n in range(2):
                columns(S_OUT_O + n, a["od_w_out"][0], 512 * n, 512)

            def expert_half(e, n, u, wait):
                h = (2 * S_MOE + u) % HALVES
                if wait:
                    sp.wait_ge(unit_done, F_UNITS + E_UNITS * n + u - HALVES + 1)
                    sp.sem_inc(halves_reused, 1)
                if u < 2 * W13_SLOTS:
                    m, k = divmod(u, 2)
                    dst = ring[:, h, :].rearrange("p (k m n) -> p k m n", k=4, m=2)
                    for i, w in enumerate((a["od_exp_w1"], a["od_exp_w3"])):
                        sp.dma_start(dst[:, :, i, :],
                                     w[0, bass.ds(e, 1), 512 * k:512 * k + 512, 256 * m:256 * m + 256]
                                     .rearrange("o (k p) n -> p (o k) n", p=P)).then_inc(half_landed[h], 16)
                else:
                    r0 = 2 * P * (u - 2 * W13_SLOTS)
                    for i in range(2):
                        sp.dma_start(ring[:, h, i * D:(i + 1) * D],
                                     a["od_exp_w2"][0, bass.ds(e, 1), r0 + i * P:r0 + (i + 1) * P, :]
                                     .rearrange("o p n -> p (o n)")).then_inc(half_landed[h], 16)

            def expert_weights(rnd):
                for u in range(HALVES):
                    if rnd == 0:
                        sp.wait_ge(*read(S_MOE - RING + u // 2))
                    expert_half(0, NE * rnd, u, rnd > 0)
                with sp.Fori(0, NE - 1) as e:
                    for u in range(HALVES, E_UNITS):
                        expert_half(e, e + NE * rnd, u, True)
                    for u in range(HALVES):
                        expert_half(e + 1, e + 1 + NE * rnd, u, True)
                for u in range(HALVES, E_UNITS):
                    expert_half(NE - 1, NE - 1 + NE * rnd, u, True)

            expert_weights(0)
            sp.wait_ge(flag_ready, 1)
            crowded = sp.value_load(flag[0:1, 0:1], min_val=0, max_val=1)
            with sp.If(crowded > 0):
                expert_weights(1)
            for t in range(LAT_TILES):
                sp.wait_ge(final_ready, 2 * (t + 1))
                sp.dma_start(out[0, t * P:(t + 1) * P, :], X[:, t, :]).then_inc(out_done, 16)
            sp.wait_ge(out_done, 16 * LAT_TILES)

        @block.tensor
        def _(pe):
            def modulation():
                pe.wait_ge(cond_ready, 1)
                pe.wait_ge(cst_landed, 16)
                for n in range(13):
                    if n < 12:
                        wait_slot(pe, n)
                        if n >= 2:
                            pe.wait_ge(mod_row, n - 1)
                        w = slot(n).rearrange("p (k n) -> p k n", k=DC)
                        for c in range(DC):
                            mm = pe.matmul(bank[n % 2][0:2, :], silc[:, c, :], w[:, c, :],
                                           start=(c == 0), stop=(c == DC - 1))
                        mm.then_inc(mod_psum, 1)
                    if n >= 1:
                        pe.wait_ge(mod_row, n)
                        for j in range(4):
                            col = 8 * (n - 1) + 2 * j
                            mm = pe.transpose(bank[2][:, col:col + 2], mrow[0:2, (n - 1) % 2, j * P:(j + 1) * P],
                                              ident[0:2, 0:2])
                        if n == 12:
                            mm.then_inc(mod_turned, 1)

            def modulation_part(n, chunks):
                if chunks[0] == 0:
                    if n == 0:
                        pe.wait_ge(four_o, 8)
                    wait_slot(pe, S_MOD[1] + n)
                    pe.wait_ge(mod_row, 12 + n)
                w = slot(S_MOD[1] + n).rearrange("p (k n) -> p k n", k=DC)
                for c in chunks:
                    mm = pe.matmul(bank[7][0:2, :], silc[:, c, :], w[:, c, :], start=(c == 0), stop=(c == DC - 1))
                if chunks[-1] == DC - 1:
                    mm.then_inc(mod_psum, 1)

            def modulation_turn():
                pe.wait_ge(mod_row, 24)
                for j in range(48):
                    mm = pe.transpose(bank[2][:, 2 * j:2 * j + 2], rows[0:2, j * P:(j + 1) * P], ident[0:2, 0:2])
                mm.then_inc(mod_turned, 1)

            def norm_turn(q):
                tiles = NORMS[q][3]
                pe.wait_ge(xn_ready, sum(NORMS[i][3] for i in range(q + 1)))
                for c in range(DC):
                    k = DC * q + c
                    if k == 2:
                        pe.wait_ge(coef_ready, 1)
                    if k >= 4:
                        pe.wait_ge(ht_act if k % 2 == 0 else ht_dve, k // 2 - 1)
                    for t in range(tiles):
                        mm = pe.transpose(bank[k % 4][:, t * P:(t + 1) * P], XN(q)[:, t, c * P:(c + 1) * P], ident)
                    mm.then_inc(xn_turned, 1)

            def wait_ht(q):
                pe.wait_ge(ht_act, DC // 2 * (q + 1))
                pe.wait_ge(ht_dve, DC // 2 * (q + 1))

            def w_in_even():
                wait_ht(0)
                for j in range(16):
                    n, t = divmod(j, 4)
                    if t == 0:
                        wait_slot(pe, S_IN_E + n)
                    if j >= 4:
                        if (j - 4) // 4 in (0, 3):
                            pe.wait_ge(in_copied, j - 3)
                        else:
                            pe.wait_ge(in_normed, j - 4 - 3)
                    w = slot(S_IN_E + n).rearrange("p (k n) -> p k n", k=DC)
                    for c in range(DC):
                        mm = pe.matmul(bank[4 + j % 4][:, :], hT[:, c, t * P:(t + 1) * P], w[:, c, :],
                                       start=(c == 0), stop=(c == DC - 1))
                    mm.then_inc(in_psum, 1)

            def qk_turn_even():
                for j in range(8):
                    n, c = divmod(j, 4)
                    if c == 0:
                        pe.wait_ge(head_ready, 4 * (n + 1))
                    if j >= 2:
                        pe.wait_ge(qk_act if j % 2 == 0 else qk_dve, j // 2)
                    for t in range(TILES):
                        mm = pe.transpose(bank[j % 2][:, t * P:(t + 1) * P],
                                          hn[:, 1 + n, t, c * P:(c + 1) * P], ident)
                    mm.then_inc(qk_turned, 1)

            def fourier():
                pe.wait_ge(in_copied, 8)
                pe.wait_ge(in_normed, 8)
                pe.wait_ge(dft_landed, 16)
                for u in range(9):
                    if u < 8:
                        s, g = divmod(u, 4)
                        if u >= 2:
                            pe.wait_ge(four_t, u - 1)
                        for k in range(2):
                            mm = pe.matmul(bank[4 + u % 2][:, :], hn[:, 0, 2 * s + k, g * P:(g + 1) * P],
                                           dft[:, k * 512:(k + 1) * 512], start=(k == 0), stop=(k == 1))
                        mm.then_inc(four_a, 1)
                    if u >= 1:
                        v = u - 1
                        pe.wait_ge(four_t, v + 1)
                        if v >= 2:
                            pe.wait_ge(four_o, v - 1)
                        for k in range(2):
                            mm = pe.matmul(bank[6 + v % 2][:, 0:SEQ], dft[:, 1024 + k * P:1024 + (k + 1) * P],
                                           T1[:, v % 2, k * SEQ:(k + 1) * SEQ], start=(k == 0), stop=(k == 1))
                        mm.then_inc(four_b, 1)

            def attention(jobs, j0):
                n = len(jobs)
                for r in range(n + 3):
                    i = j0 + r
                    if r < n:
                        qa, ka, keys = jobs[r][0:3]
                        if i >= 3:
                            pe.wait_ge(exp_done, i - 2)
                        pe.matmul(bank[i % 3][:, 0:keys], qa, ka, start=True, stop=True).then_inc(scores, 1)
                        if jobs is EVEN_JOBS:
                            modulation_part(*MOD_FILL[r])
                    if 2 <= r < n + 2:
                        k = i - 2
                        pe.wait_ge(prob_ready, k + 1)
                        if k >= 2:
                            pe.wait_ge(pt_ready, k - 1)
                        for c in range(jobs[r - 2][2] // P):
                            mm = pe.transpose(bank[3 + k % 2][:, c * P:(c + 1) * P],
                                              prob[:, k % 3, c * P:(c + 1) * P], ident)
                        mm.then_inc(prob_turned, 1)
                    if r >= 4 and r % 2 == 0:
                        pe_pv(jobs, r - 3, i - 3)

            def pe_pv(jobs, r, i):
                keys, vs, half = jobs[r][2], jobs[r][3], jobs[r][4]
                pe.wait_ge(pt_ready, i + 1)
                h = i // 2
                if h >= 2:
                    pe.wait_ge(o_ready, h - 1)
                for k in range(keys // P):
                    mm = pe.matmul(bank[5 + h % 2][64 * half:64 * half + HD, 0:SEQ], vs[k], pT[:, h % 2, k, :],
                                   start=(k == 0), stop=(k == keys // P - 1))
                mm.then_inc(o_psum, 1)

            def gate_rows(q):
                layer, m, streams = GATES[q]
                k = 2 * sum(GATES[i][2] for i in range(q))
                for s in range(streams):
                    for half in range(2):
                        if k >= 1:
                            pe.wait_ge(gate_ready, k)
                        else:
                            pe.wait_ge(four_o, 8)
                        for j in range(4):
                            c = m + 4 * half + j
                            mm = pe.matmul(bank[7][:, j * P:(j + 1) * P],
                                           mod[layer][:, c, s:s + 1].to_broadcast([P, P]), ident,
                                           start=True, stop=True)
                        mm.then_inc(gate_psum, 1)
                        k += 1

            def w_out(slot0, tiles, oTv, r0):
                for half in range(2):
                    wait_slot(pe, slot0 + half)
                    w = slot(slot0 + half).rearrange("p (k n) -> p k n", k=DC)
                    for t in range(tiles):
                        r = r0 + half * tiles + t
                        if half * tiles + t >= 4:
                            pe.wait_ge(res_gated, r - 3)
                        for c in range(DC):
                            mm = pe.matmul(bank[3 + (half * tiles + t) % 4][:, :], oTv[:, c, t * P:(t + 1) * P],
                                           w[:, c, :], start=(c == 0), stop=(c == DC - 1))
                        mm.then_inc(res_psum, 1)

            def dense_swiglu(r0):
                for u, what in enumerate(F_ORDER):
                    pe.wait_ge(split_lo, u + 1)
                    if what[0] == "up":
                        n, m = what[1:]
                        w = [part(i, 2 * S_FFN + u).rearrange("p (k n) -> p k n", k=DC) for i in range(2)]
                        if u == 1:
                            pe.wait_ge(mod_ready, 1)
                        if n:
                            pe.wait_ge(up_silu if m == 0 else g_full, 2 * n)
                        if u and F_ORDER[u - 1][0] == "down":
                            q = F_ORDER[u - 1][1]
                            pe.wait_ge(res_gated, r0 + 8 * (q + 1))
                        for f in range(2):
                            for c in range(DC):
                                if u == 0 and f == 0:
                                    pe.wait_ge(ht_lo, c + 1)
                                for x, (i, j) in enumerate(PASSES):
                                    mm = pe.matmul(bank[2 * m + f][:, :], w[i][:, c, f * P:(f + 1) * P],
                                                   hTr[:, j, c, :], start=(c == 0 and x == 0),
                                                   stop=(c == DC - 1 and x == 2))
                    else:
                        q, d, kh = what[1:]
                        k0, ks = sum(FG[:q]), FG[q] // 2
                        w = [part(i, 2 * S_FFN + u, ks * 512).rearrange("p (k n) -> p k n", k=ks) for i in range(2)]
                        if kh == 0:
                            if d == 0 and q:
                                pe.wait_ge(res_gated, r0 + 8 * q - 4)
                            if d == 1:
                                pe.wait_ge(g_full, k0 + FG[q])
                        for k in range(ks):
                            c = ks * kh + k
                            if d == 0:
                                pe.wait_ge(g_lo, k0 + c + 1)
                            for t in range(TILES):
                                for x, (i, j) in enumerate(PASSES):
                                    mm = pe.matmul(bank[t + (4 if d == 0 else 0)][:, :],
                                                   gTr[:, i, c, t * P:(t + 1) * P], w[j][:, k, :],
                                                   start=(c == 0 and x == 0), stop=(c == FG[q] - 1 and x == 2))
                    mm.then_inc(unit_done, 1)

            modulation()
            norm_turn(0)
            w_in_even()
            qk_turn_even()
            fourier()
            pe.wait_ge(qk_act, 4)
            pe.wait_ge(qk_dve, 4)
            attention(EVEN_JOBS, 0)
            modulation_turn()
            gate_rows(0)
            pe.wait_ge(o_ready, len(EVEN_JOBS) // 2)
            pe.wait_ge(four_o, 8)
            w_out(S_OUT_E, 4, oT, 0)
            norm_turn(1)
            gate_rows(1)
            dense_swiglu(8)

            def w_in_odd():
                wait_ht(2)
                for i, (n, t) in enumerate(IN_JOBS):
                    if t == 0:
                        wait_slot(pe, S_IN_O + n)
                    if i >= 4:
                        pe.wait_ge(*((in_normed, i + 5) if i - 4 < 8 else (in_copied, i + 1)))
                    w_ = IN_COLS[n][1]
                    w = slot(S_IN_O + n)[:, 0:DC * w_].rearrange("p (k n) -> p k n", k=DC)
                    for c in range(DC):
                        mm = pe.matmul(bank[4 + i % 4][:, 0:w_], hT[:, c, t * P:(t + 1) * P], w[:, c, :],
                                       start=(c == 0), stop=(c == DC - 1))
                    mm.then_inc(in_psum, 1)

            def turn_odd():
                for jj in range(10):
                    j = 8 + jj
                    if jj == 0:
                        pe.wait_ge(head_ready, 12)
                    if jj == 3:
                        pe.wait_ge(head_ready, 16)
                    if jj == 6:
                        pe.wait_ge(in_copied, 16)
                    pe.wait_ge(qk_act if j % 2 == 0 else qk_dve, j // 2)
                    for t in range(4):
                        o = bank[j % 2][:, t * P:(t + 1) * P]
                        if jj < 3:
                            mm = pe.transpose(o, qn[:, t % 2, (2 * jj + t // 2) * P:(2 * jj + t // 2 + 1) * P], ident)
                        elif jj < 6:
                            mm = pe.transpose(o, kn[:, t, jj - 3, :, :].rearrange("p b d -> p (b d)"), ident)
                        elif jj < 8:
                            mm = pe.transpose(o, un[:, (t + 2) % 4, (jj - 6) * P:(jj - 5) * P], ident)
                        else:
                            mm = pe.matmul(o, un[:, 3 - t, (jj - 8) * P:(jj - 7) * P], rev,
                                           start=True, stop=True)
                    mm.then_inc(qk_turned, 1)

            def s5():
                pe.wait_ge(s5_bbar, 1)
                pe.wait_ge(in_normed, 16)
                for i in range(2):
                    for g in range(4):
                        mm = pe.transpose(bank[2 + i][:, g * P:(g + 1) * P],
                                          b_bar[i][:, 4 * g:4 * g + 4, :].rearrange("p u n -> p (u n)"), ident)
                    mm.then_inc(s5_turned, 1)
                pe.wait_ge(s5_bt_act, 1)
                pe.wait_ge(s5_bt_dve, 1)
                pe.wait_ge(qk_act, 9)
                pe.wait_ge(qk_dve, 9)
                pe.wait_ge(s5_c, 2)
                for k in range(UNITS + 1):
                    if k < UNITS:
                        j, d = divmod(k, 2)
                        g, r = 2 * d + j // 4, 32 * (j % 4)
                        if k >= 2:
                            pe.wait_ge(s5_bu_used, k - 1)
                        for i in range(2):
                            mm = pe.matmul(bank[2 * (k % 2) + i][:, :], BT[i][r:r + 32, g * P:(g + 1) * P],
                                           uT[d][r:r + 32, j // 4, :], start=True, stop=True)
                        mm.then_inc(s5_bu, 1)
                    if k >= 1:
                        j, d = divmod(k - 1, 2)
                        r, u = 32 * (j % 4), PAIRS * d + j
                        pe.wait_ge(s5_s, k)
                        for i, c in enumerate((C5[0], C5neg, C5[1], C5[1])):
                            mm = pe.matmul(bank[4 + j // 4][r:r + 32, 0:SEQ], c[:, u, :],
                                           s_out[:, (k - 1) % 2, i, :], start=(d == 0 and i == 0),
                                           stop=(d == 1 and i == 3))
                        mm.then_inc(s5_y, 1)
                pe.wait_ge(glu_landed, 16)
                pe.wait_ge(y5_gelu, 1)
                for m in range(2):
                    for k in range(2):
                        mm = pe.matmul(bank[6][:, m * SEQ:(m + 1) * SEQ], gluw[:, k, m * P:(m + 1) * P], y5s[:, k, :],
                                       start=(k == 0), stop=(k == 1))
                mm.then_inc(glu_psum, 1)

            norm_turn(2)
            w_in_odd()
            turn_odd()
            s5()
            pe.wait_ge(ssm_ready, 1)
            attention(ODD_JOBS, ATTN_E)
            gate_rows(2)
            pe.wait_ge(o_ready, len(EVEN_JOBS) // 2 + len(ODD_JOBS) // 2)
            w_out(S_OUT_O, 2, oTo, 8 + RES_FFN)
            norm_turn(3)
            gate_rows(3)

            wait_ht(3)
            for t in range(2):
                for c in range(DC):
                    mm = pe.matmul(bank[2][:, 8 * t:8 * t + 8], hT[:, c, t * P:(t + 1) * P],
                                   vec[:, V_RW + 8 * c:V_RW + 8 * c + 8], start=(c == 0), stop=(c == DC - 1))
            mm.then_inc(logits, 1)
            pe.wait_ge(sel_ready, 1)
            tri, one = cst[:, C_TRI:C_TRI + P], cst[:, C_ONE:C_ONE + P]
            sel = s5v[:, R_SEL, :]
            for o, parts in ((0, [(tri, 0)]), (8, [(one, 0), (tri, 1)]), (16, [(one, 0), (one, 1)])):
                for k, (m, t) in enumerate(parts):
                    mm = pe.matmul(bank[3][:, o:o + 8], m, sel[:, 8 * t:8 * t + 8], start=(k == 0),
                                   stop=(k == len(parts) - 1))
            mm.then_inc(ranks, 1)

            def gather(e, n):
                pe.wait_ge(e_added, 4 * n + 1)
                for h in range(2):
                    for j in range(4):
                        c = 4 * h + j
                        for t in range(2):
                            mm = pe.matmul(bank[6 + h][:, j * P:(j + 1) * P], xn[:, t, c * P:(c + 1) * P],
                                           pick[:, t, bass.ds(e, 1), :].rearrange("p o s -> p (o s)"),
                                           start=(t == 0), stop=(t == 1))
                    mm.then_inc(e_gather, 1)

            def turn_hidden(n, m):
                pe.wait_ge(e_gated, 2 + W13_SLOTS * n + m + 1)
                pe.wait_ge(heT_lo, W13_SLOTS * n + m + 1)
                for j in range(2):
                    mm = pe.transpose(bank[2 + m % 2][:, j * P:(j + 1) * P], he[:, m % 2, j * P:(j + 1) * P], ident)
                mm.then_inc(e_turned, 1)

            def expert(e, rnd):
                n = e + NE * rnd
                g = F_UNITS + E_UNITS * n
                pe.wait_ge(xe_lo, n + 1 + rnd)
                for u in range(E_UNITS):
                    pe.wait_ge(split_lo, g + u + 1)
                    w = [part(i, 2 * S_MOE + u) for i in range(2)]
                    if u < 2 * W13_SLOTS:
                        m, kh = divmod(u, 2)
                        if kh == 0:
                            pe.wait_ge(e_gated, W13_SLOTS * n + m + 1)
                        for k in range(4):
                            for x, (i, j) in enumerate(PASSES):
                                mm = pe.matmul(bank[m % 2][:, :], xer[:, i, 4 * kh + k, :],
                                               w[j][:, 512 * k:512 * k + 512],
                                               start=(kh == 0 and k == 0 and x == 0),
                                               stop=(kh == 1 and k == 3 and x == 2))
                        mm.then_inc(unit_done, 1)
                        if kh == 1 and m >= 1:
                            turn_hidden(n, m - 1)
                    else:
                        v = u - 2 * W13_SLOTS
                        pe.wait_ge(heT_lo, 2 + W13_SLOTS * n + v + 1)
                        for k in range(2):
                            c = 2 * v + k
                            for h in range(2):
                                for x, (i, j) in enumerate(PASSES):
                                    mm = pe.matmul(bank[4 + h][:, :], heTr[:, i, c, :],
                                                   w[j][:, D * k + 512 * h:D * k + 512 * h + 512],
                                                   start=(c == 0 and x == 0), stop=(c == EC - 1 and x == 2))
                        mm.then_inc(unit_done, 1)
                        if v == 0:
                            turn_hidden(n, W13_SLOTS - 1)
                        if v == GATHER_AT:
                            gather(e + 1, n)
                pe.wait_ge(y_act, n + 1)
                pe.wait_ge(y_dve, n + 1)
                pe.wait_ge(gte_ready, n + 1)
                for k in range(4):
                    h, t = divmod(k, 2)
                    if k < 2:
                        pe.wait_ge(xf_act if k == 0 else xf_dve, n + 2 + rnd)
                    else:
                        pe.wait_ge(e_added, 4 * n + k)
                    pe.matmul(bank[6 + k % 2][:, :], gTe[:, t * P:(t + 1) * P], ye[:, h * 512:(h + 1) * 512],
                              start=True, stop=True).then_inc(e_scatter, 1)

            def experts(rnd):
                pe.wait_ge(pick_ready, 2 * rnd + 1)
                if rnd == 0:
                    pe.wait_ge(gate_ready, 12)
                gather(0, NE * rnd)
                pe.wait_ge(pick_ready, 2 * rnd + 2)
                for g in range(4):
                    for j in range(2):
                        for t in range(2):
                            mm = pe.transpose(bank[2 + g][:, (2 * j + t) * P:(2 * j + t + 1) * P],
                                              gpick[:, t, 2 * g + j, :], ident)
                    mm.then_inc(gpick_turned, 1)
                pe.wait_ge(gta_act, 2 * (rnd + 1))
                pe.wait_ge(gta_dve, 2 * (rnd + 1))
                with pe.Fori(0, NE) as e:
                    expert(e, rnd)

            experts(0)
            pe.wait_ge(flag_ready, 1)
            crowded = pe.value_load(flag[0:1, 0:1], min_val=0, max_val=1)
            with pe.If(crowded > 0):
                experts(1)

        @block.scalar
        def _(act):
            act.dma_start(vec[:, :], a["vec"]).then_inc(vec_landed, 16)
            act.dma_start(cst[:, :], a["cst"]).then_inc(cst_landed, 16)
            act.dma_start(X[:, 0:2, :], a["x"][0].rearrange("(t p) d -> p t d", p=P)).then_inc(x_landed, 16)
            act.dma_start(X[:, 2:4, :], a["ctx"][0].rearrange("(t p) d -> p t d", p=P)).then_inc(x_landed, 16)
            act.dma_start(dft, a["dft"]).then_inc(dft_landed, 16)
            act.wait_ge(vec_landed, 16)
            act.activation(silc[:, :, :], vec[:, V_COND:V_COND + 16].rearrange("p (k s) -> p k s", s=2),
                           ACT.Silu).then_inc(cond_ready, 1)

            roots = [0]

            def root(v):
                roots[0] += 1
                act.wait_ge(mean_ready, roots[0])
                act.activation(v, v, ACT.Sqrt).then_inc(root_ready, 1)

            def squares(q):
                tiles, before = NORMS[q][3:5]
                if q == 0:
                    act.wait_ge(x_landed, 32)
                else:
                    act.wait_ge(res_done, before)
                for t in range(tiles):
                    act.activation(XN(q)[:, t, :], X[:, t, :], ACT.Square,
                                   accum_out=ss[:, t:t + 1]).then_inc(square_sum, 1)
                root(rstd[:, 0:tiles])

            def modulate(q):
                layer, sh, sc = NORMS[q][0:3]
                act.wait_ge(coef_ready, q + 1)
                for c in range(0, DC, 2):
                    act.wait_ge(xn_turned, DC * q + c + 1)
                    if q == 1 and c >= 4:
                        act.wait_ge(ht_lo, c - 3)
                    dst = hf[:, c % 4, :] if q == 1 else hT[:, c, :]
                    for s in range(NORMS[q][3] // 2):
                        ins = act.activation(dst[:, s * SEQ:(s + 1) * SEQ], bank[c % 4][:, s * SEQ:(s + 1) * SEQ],
                                             ACT.Identity, bias=mod[layer][:, sh + c, s:s + 1],
                                             scale=coef[:, q, c, s:s + 1])
                    ins.then_inc(ht_act, 1)
                    for cc in (c, c + 1) if q == 1 else ():
                        act.wait_ge(ht_act if cc == c else ht_dve, (DC + cc) // 2 + 1)
                        act.activation(hTr[:, 0, cc, :], hf[:, cc % 4, :], ACT.Copy).then_inc(ht_hi, 1)

            squares(0)
            modulate(0)
            for j in range(16):
                n, t = divmod(j, 4)
                act.wait_ge(in_psum, j + 1)
                if n in (0, 3):
                    act.activation(hn[:, n, t, :], bank[4 + j % 4][:, :], ACT.Copy).then_inc(in_copied, 1)
                else:
                    if j - 4 >= 2:
                        act.wait_ge(in_summed, j - 5)
                    act.activation(sq[:, j % 2, :], bank[4 + j % 4][:, :], ACT.Square).then_inc(in_squared, 1)
                    root(hss[:, 0:8])
            for j in range(0, 8, 2):
                act.wait_ge(qk_turned, j + 1)
                act.activation(hT[:, j, :], bank[0][:, :], ACT.Copy).then_inc(qk_act, 1)
            for u in range(8):
                act.wait_ge(four_a, u + 1)
                if u >= 2:
                    act.wait_ge(four_b, u - 1)
                act.activation(T1[:, u % 2, :], bank[4 + u % 2][:, :], ACT.Copy).then_inc(four_t, 1)

            def attention(jobs, j0):
                n = len(jobs)
                for r in range(n + 3):
                    i = j0 + r
                    if r < n:
                        keys = jobs[r][2]
                        act.wait_ge(row_max, i + 1)
                        if i >= 3:
                            act.wait_ge(prob_turned, i - 2)
                        act.activation(prob[:, i % 3, 0:keys], bank[i % 3][:, 0:keys], ACT.Exp,
                                       bias=nmax[:, i % 4:i % 4 + 1],
                                       accum_out=rsum[:, i % 4:i % 4 + 1]).then_inc(exp_done, 1)
                    if r >= 3:
                        keys = jobs[r - 3][2]
                        k = i - 3
                        act.wait_ge(prob_turned, k + 1)
                        if k // 2 >= 2:
                            act.wait_ge(o_psum, k // 2 - 1)
                        act.activation(pT[:, (k // 2) % 2, 0:keys // P, (k % 2) * P:(k % 2 + 1) * P],
                                       bank[3 + k % 2][:, 0:keys].rearrange("p (k q) -> p k q", q=P),
                                       ACT.Copy).then_inc(pt_ready, 1)

            def gate_rows(q):
                layer, m, streams = GATES[q]
                k = 2 * sum(GATES[i][2] for i in range(q))
                if q:
                    act.wait_ge(res_gated, [0, 8, 8 + RES_FFN, 12 + RES_FFN][q])
                if q % 2 == 0:
                    act.wait_ge(prob_turned, len(EVEN_JOBS) + (len(ODD_JOBS) if q else 0))
                for s in range(streams):
                    for half in range(2):
                        act.wait_ge(gate_psum, k + 1)
                        g = (G[:, s, :], GF[:, s, :], G[:, s, :], G2)[q]
                        act.activation(g[:, half * 512:(half + 1) * 512], bank[7][:, :],
                                       ACT.Copy).then_inc(gate_ready, 1)
                        k += 1

            attention(EVEN_JOBS, 0)
            gate_rows(0)

            def split(g, h):
                act.wait_ge(half_landed[h % HALVES], 32 * (h // HALVES + 1))
                if g >= HALVES:
                    act.wait_ge(unit_done, g - HALVES + 1)
                n = unit_width(g)
                act.activation(part(0, h, n), ring[:, h % HALVES, 0:n], ACT.Copy).then_inc(split_hi, 1)

            act.wait_ge(mod_turned, 2)
            for g in range(2):
                split(g, 2 * S_FFN + g)
            squares(1)
            modulate(1)
            gate_rows(1)
            for g in range(2, AHEAD):
                split(g, 2 * S_FFN + g)
            for u, what in enumerate(F_ORDER):
                if u + AHEAD < F_UNITS:
                    split(u + AHEAD, 2 * S_FFN + u + AHEAD)
                if what[0] == "down":
                    continue
                n, m = what[1:]
                if m == 0:
                    act.wait_ge(unit_done, u + 1)
                    for f in range(2):
                        if n:
                            act.wait_ge(g_full, 2 * n)
                        act.activation(sil[:, f, :], bank[f][:, :], ACT.Silu).then_inc(up_silu, 1)
                else:
                    for f in range(2):
                        act.wait_ge(g_full, 2 * n + f + 1)
                        act.activation(gTr[:, 0, (2 * n + f) % max(FG), :], gf[:, f, :], ACT.Copy).then_inc(g_hi, 1)
            squares(2)
            act.dma_start(S[:, 5632:6656].rearrange("p (i n) -> p i n", i=2),
                          a["s5b"].rearrange("i p n -> p i n")).then_inc(s5_raw, 16)
            act.dma_start(B[:, 9984:11008].rearrange("p (i n) -> p i n", i=2),
                          a["s5c"].rearrange("i p n -> p i n")).then_inc(s5_raw, 16)
            modulate(2)
            for i, (n, t) in enumerate(IN_JOBS):
                act.wait_ge(in_psum, 16 + i + 1)
                ps = bank[4 + i % 4]
                if n == 3:
                    act.activation(un[:, t, :], ps[:, 0:256], ACT.Copy).then_inc(in_copied, 1)
                    continue
                w_ = (512, 256, 192)[n]
                if i < 2:
                    act.wait_ge(in_summed, 8)
                else:
                    act.wait_ge(in_summed, 8 + i - 1)
                act.activation(sqo[:, i % 2, 0:w_], ps[:, 0:w_], ACT.Square).then_inc(in_squared, 1)
                if n == 2:
                    act.activation(vn[:, t, :], ps[:, 192:384], ACT.Copy).then_inc(in_copied, 1)
                root(hss[:, 0:w_ // HD])
            for j in range(8, 18, 2):
                act.wait_ge(qk_turned, j + 1)
                jj = j - 8
                dst = (HT[:, 512 * jj:512 * jj + 512] if jj < 6 else uT[(jj - 6) // 2][:, jj % 2, :])
                act.activation(dst, bank[0][:, :], ACT.Copy).then_inc(qk_act, 1)
            act.dma_start(gluw, a["od_s5_glu_w"][0].rearrange("(k p) n -> p k n", p=P)).then_inc(glu_landed, 16)
            act.wait_ge(s5_turned, 1)
            act.activation(BT[0], bank[2][:, :], ACT.Copy).then_inc(s5_bt_act, 1)
            act.wait_ge(y5_ready, 1)
            act.activation(y5s[:, :, :], y5[:, :, :], ACT.Gelu_apprx_tanh).then_inc(y5_gelu, 1)
            act.wait_ge(glu_psum, 1)
            for m in range(2):
                ins = act.activation(y5[:, m, :], bank[6][:, m * SEQ:(m + 1) * SEQ], ACT.Sigmoid,
                                     bias=vec[:, V_GLUB + m:V_GLUB + m + 1])
            ins.then_inc(glu_sig, 1)
            def split_unit(n, u):
                h = 2 * S_MOE + u
                act.wait_ge(half_landed[h % HALVES], 32 * (h // HALVES + 1) + n * (32 * E_UNITS // HALVES))
                act.wait_ge(unit_done, F_UNITS + E_UNITS * n + u - HALVES + 1)
                act.activation(part(0, h), ring[:, h % HALVES, :], ACT.Copy).then_inc(split_hi, 1)

            attention(ODD_JOBS, ATTN_E)
            gate_rows(2)
            split_unit(0, 0)
            split_unit(0, 1)
            squares(3)
            modulate(3)
            gate_rows(3)
            for u in range(2, AHEAD + 1):
                split_unit(0, u)
            act.wait_ge(top_gap, 1)
            act.activation(s5v[:, R_T, 4:6], s5v[:, R_T, 2:4], ACT.Exp).then_inc(top_exp, 1)

            def tasks(n, u, rnd):
                g = F_UNITS + E_UNITS * n
                if u < 2 * W13_SLOTS and u % 2 == 1:
                    m = u // 2
                    act.wait_ge(unit_done, g + u + 1)
                    act.activation(sile[:, m % 2, :], bank[m % 2][:, 0:256], ACT.Silu).then_inc(e_silu, 1)
                    if m >= 1:
                        turned(n, m - 1)
                if u == 2 * W13_SLOTS:
                    turned(n, W13_SLOTS - 1)
                if u == 2 * W13_SLOTS + GATHER_AT:
                    gathered(n + rnd + 1)
                if u == E_UNITS - 1:
                    act.wait_ge(unit_done, g + E_UNITS)
                    act.activation(ye[:, 0:512], bank[4][:, :], ACT.Copy).then_inc(y_act, 1)

            def gathered(i):
                act.wait_ge(e_gather, 2 * i + 1)
                for c in range(4):
                    ins = act.activation(xf[:, c, :], bank[6][:, c * P:(c + 1) * P], ACT.Identity,
                                         bias=mod[1][:, M_SH2 + c, 0:1], scale=coef[:, 3, c, 0:1])
                ins.then_inc(xf_act, 1)
                act.wait_ge(xf_act, i + 1)
                act.wait_ge(xf_dve, i + 1)
                act.activation(xer[:, 0, :, :], xf[:, :, :], ACT.Copy).then_inc(xe_hi, 1)

            def turned(n, m):
                act.wait_ge(e_turned, W13_SLOTS * n + m + 1)
                act.activation(heTr[:, 0, 2 * m:2 * m + 2, :], bank[2 + m % 2][:, 0:2 * P]
                               .rearrange("p (c s) -> p c s", c=2), ACT.Copy).then_inc(heT_hi, 1)

            def expert(n, rnd, last):
                for u in range(1, E_UNITS):
                    if u + AHEAD < E_UNITS:
                        split_unit(n, u + AHEAD)
                    elif not last:
                        split_unit(n + 1, u + AHEAD - E_UNITS)
                    tasks(n, u, rnd)
                if not last:
                    split_unit(n + 1, AHEAD)

            def experts(rnd):
                for g in range(0, 4, 2):
                    act.wait_ge(gpick_turned, 4 * rnd + g + 1)
                    act.activation(gTall[:, 2 * g:2 * g + 2, :].rearrange("p e t -> p (e t)"), bank[2 + g][:, :],
                                   ACT.Copy).then_inc(gta_act, 1)
                gathered((NE + 1) * rnd)
                for u in range(AHEAD + 1) if rnd else ():
                    split_unit(NE * rnd, u)
                with act.Fori(0, NE - 1) as e:
                    expert(e + NE * rnd, rnd, False)
                expert(NE - 1 + NE * rnd, rnd, True)

            experts(0)
            act.wait_ge(flag_ready, 1)
            crowded = act.value_load(flag[0:1, 0:1], min_val=0, max_val=1)
            with act.If(crowded > 0):
                experts(1)

        @block.vector
        def _(dve):
            steps = [0]

            def step(ins):
                steps[0] += 1
                ins.then_inc(dve_step, 1)
                dve.wait_ge(dve_step, steps[0])

            roots = [0]

            def rsqrt_mean(o, sums, n):
                roots[0] += 1
                dve.tensor_scalar(o, sums, 1.0 / n, EPS, ALU.mult, ALU.add).then_inc(mean_ready, 1)
                dve.wait_ge(root_ready, roots[0])
                step(dve.reciprocal(o, o))

            def modulation_rows(n):
                dve.wait_ge(mod_psum, 12 + n + 1)
                dve.tensor_copy(rows[0:2, 512 * n:512 * (n + 1)], bank[7][0:2, :]).then_inc(mod_row, 1)

            def modulated(layer):
                dve.wait_ge(mod_turned, layer + 1)
                b = vec[:, V_MODB + 48 * layer:V_MODB + 48 * layer + 48]
                step(dve.tensor_tensor(mod[layer][:, :, :], bank[2][:, 0:96].rearrange("p (c s) -> p c s", s=2),
                                       b.unsqueeze(2).to_broadcast([P, 48, 2]), ALU.add))
                for q in (2 * layer, 2 * layer + 1):
                    sc = NORMS[q][2]
                    gain = vec[:, V_NORM + DC * q:V_NORM + DC * q + DC]
                    step(dve.tensor_scalar(coef[:, q], mod[layer][:, sc:sc + DC, :], 1.0, None, ALU.add))
                    dve.tensor_tensor(coef[:, q], coef[:, q], gain.unsqueeze(2).to_broadcast([P, DC, 2]),
                                      ALU.mult).then_inc(coef_ready, 1)
                dve.wait_ge(coef_ready, 2 * layer + 2)
                if layer:
                    dve.sem_inc(mod_ready, 1)

            def normed(q):
                tiles = NORMS[q][3]
                dve.wait_ge(square_sum, sum(NORMS[i][3] for i in range(q + 1)))
                rsqrt_mean(rstd[:, 0:tiles], ss[:, 0:tiles], D)
                for t in range(tiles):
                    dve.tensor_scalar(XN(q)[:, t, :], X[:, t, :], rstd[:, t:t + 1], None,
                                      ALU.mult).then_inc(xn_ready, 1)

            def modulate(q):
                layer, sh = NORMS[q][0:2]
                for c in range(1, DC, 2):
                    dve.wait_ge(xn_turned, DC * q + c + 1)
                    if q == 1 and c >= 4:
                        dve.wait_ge(ht_lo, c - 3)
                    dst = hf[:, c % 4, :] if q == 1 else hT[:, c, :]
                    for s in range(NORMS[q][3] // 2):
                        ins = dve.tensor_scalar(dst[:, s * SEQ:(s + 1) * SEQ], bank[c % 4][:, s * SEQ:(s + 1) * SEQ],
                                                coef[:, q, c, s:s + 1], mod[layer][:, sh + c, s:s + 1],
                                                ALU.mult, ALU.add)
                    ins.then_inc(ht_dve, 1)
                    for cc in (c - 1, c) if q == 1 else ():
                        dve.wait_ge(ht_hi, cc + 1)
                        dve.tensor_tensor(hTr[:, 1, cc, :], hf[:, cc % 4, :], hTr[:, 0, cc, :].bitcast(F32),
                                          ALU.subtract).then_inc(ht_lo, 1)

            def gated_sum(half_tiles, r0, banks, buf, gate, wait):
                dve.wait_ge(gate_ready, wait)
                for k, (half, t) in enumerate(half_tiles):
                    r = r0 + k
                    if buf is tmp:
                        dve.wait_ge(res_psum, (r if r < 8 else r - RES_FFN) + 1)
                    if r >= 2:
                        dve.wait_ge(res_done, r - 1)
                    dve.tensor_tensor(buf[:, r % 2, :], bank[banks[k]][:, :],
                                      gate[:, t // 2, half * 512:(half + 1) * 512], ALU.mult).then_inc(res_gated, 1)

            dve.wait_ge(vec_landed, 16)
            are, aim = vec[:, V_ARE:V_ARE + 16], vec[:, V_AIM:V_AIM + 16]
            dve.tensor_tensor(s5v[:, 1, :], are, are, ALU.mult)
            step(dve.tensor_tensor(s5v[:, 2, :], aim, aim, ALU.mult))
            step(dve.tensor_tensor(s5v[:, 1, :], s5v[:, 1, :], s5v[:, 2, :], ALU.add))
            dve.reciprocal(s5v[:, 1, :], s5v[:, 1, :]).then_inc(s5_rden, 1)
            for hg in (H_EQ, H_OQ):
                g = vec[:, V_HEAD + hg * HD:V_HEAD + (hg + 1) * HD]
                step(dve.tensor_scalar(g, g, HD ** -0.5, None, ALU.mult))
            normed(0)
            for n in range(12):
                dve.wait_ge(mod_psum, n + 1)
                dve.tensor_copy(mrow[0:2, n % 2, :], bank[n % 2][0:2, :]).then_inc(mod_row, 1)
            modulated(0)
            modulate(0)
            for j in range(4, 12):
                n, t = divmod(j, 4)
                dve.wait_ge(in_squared, j - 3)
                dve.tensor_reduce(hss[:, 0:8], sq[:, j % 2, :].rearrange("p (h d) -> p h d", d=HD), AX,
                                  ALU.add).then_inc(in_summed, 1)
                dve.wait_ge(in_summed, j - 3)
                rsqrt_mean(hss[:, 0:8], hss[:, 0:8], HD)
                dve.tensor_tensor(hn[:, n, t, :].rearrange("p (h d) -> p h d", d=HD),
                                  bank[4 + j % 4][:, :].rearrange("p (h d) -> p h d", d=HD),
                                  hss[:, 0:8].unsqueeze(2).to_broadcast([P, 8, HD]), ALU.mult).then_inc(in_normed, 1)
                dve.wait_ge(in_normed, j - 3)
            for j in range(1, 8, 2):
                dve.wait_ge(qk_turned, j + 1)
                dve.tensor_copy(hT[:, j, :], bank[1][:, :]).then_inc(qk_dve, 1)
            for u in range(8):
                s, g = divmod(u, 4)
                dve.wait_ge(four_b, u + 1)
                if u == 0:
                    dve.wait_ge(qk_turned, 8)
                dve.tensor_copy(oT[:, g, s * SEQ:(s + 1) * SEQ], bank[6 + u % 2][:, 0:SEQ]).then_inc(four_o, 1)

            def attention(jobs, j0, oTv, c0):
                n = len(jobs)
                for r in range(n + 4):
                    i = j0 + r
                    if jobs is EVEN_JOBS and 1 <= r <= n and MOD_FILL[r - 1][1][-1] == DC - 1:
                        modulation_rows(MOD_FILL[r - 1][0])
                    if r < n:
                        keys, h, s = jobs[r][2], jobs[r][5], jobs[r][6]
                        sc = bank[i % 3]
                        dve.wait_ge(scores, i + 1)
                        if jobs is EVEN_JOBS and s == 0:
                            dve.wait_ge(bias_ready, h + 1)
                            dve.tensor_tensor(sc[:, 0:SEQ], sc[:, 0:SEQ], bias[:, h % 2, (r % 2) * SEQ:(r % 2 + 1) * SEQ],
                                              ALU.add).then_inc(bias_used, 1)
                            dve.wait_ge(bias_used, i + 1)
                        if i >= 4:
                            dve.wait_ge(exp_done, i - 3)
                        dve.tensor_reduce(nmax[:, i % 4:i % 4 + 1], sc[:, 0:keys], AX, ALU.max,
                                          negate=True).then_inc(row_max, 1)
                    if 1 <= r <= n:
                        k = i - 1
                        keys = jobs[r - 1][2]
                        dve.wait_ge(exp_done, k + 1)
                        step(dve.reciprocal(rinv[:, k % 4:k % 4 + 1], rsum[:, k % 4:k % 4 + 1]))
                        dve.tensor_scalar(prob[:, k % 3, 0:keys], prob[:, k % 3, 0:keys], rinv[:, k % 4:k % 4 + 1],
                                          None, ALU.mult).then_inc(prob_ready, 1)
                    if r >= 5 and r % 2 == 1:
                        head_out(jobs, (r - 5) // 2, (i - 5) // 2, oTv, c0)

            def head_out(jobs, hr, h, oTv, c0):
                half, head, s = jobs[2 * hr][4:7]
                dve.wait_ge(o_psum, h + 1)
                dve.tensor_copy(oTv[64 * half:64 * half + HD, c0 + head // 2, s * SEQ:(s + 1) * SEQ],
                                bank[5 + h % 2][64 * half:64 * half + HD, 0:SEQ]).then_inc(o_ready, 1)

            attention(EVEN_JOBS, 0, oT, 4)
            halves4 = [(half, t) for half in range(2) for t in range(4)]
            modulated(1)
            def split(g):
                h, n = 2 * S_FFN + g, unit_width(g)
                dve.wait_ge(split_hi, g + 1)
                dve.tensor_tensor(part(1, h, n), ring[:, h % HALVES, 0:n], part(0, h, n).bitcast(F32),
                                  ALU.subtract).then_inc(split_lo, 1)

            gated_sum(halves4[:2], 0, [3, 4], tmp, G, 4)
            split(0)
            gated_sum(halves4[2:4], 2, [5, 6], tmp, G, 4)
            split(1)
            gated_sum(halves4[4:], 4, [3, 4, 5, 6], tmp, G, 4)
            normed(1)
            modulate(1)
            for g in range(2, AHEAD):
                split(g)
            for u, what in enumerate(F_ORDER):
                if u + AHEAD < F_UNITS:
                    split(u + AHEAD)
                if what[0] == "up" and what[2] == 1:
                    n = what[1]
                    dve.wait_ge(unit_done, u + 1)
                    dve.wait_ge(up_silu, 2 * n + 2)
                    if n:
                        dve.wait_ge(g_lo, 2 * n)
                    for f in range(2):
                        dve.tensor_tensor(gf[:, f, :], sil[:, f, :], bank[2 + f][:, :], ALU.mult).then_inc(g_full, 1)
                    for f in range(2):
                        c = (2 * n + f) % max(FG)
                        dve.wait_ge(g_hi, 2 * n + f + 1)
                        dve.tensor_tensor(gTr[:, 1, c, :], gf[:, f, :], gTr[:, 0, c, :].bitcast(F32),
                                          ALU.subtract).then_inc(g_lo, 1)
                if what[0] == "down" and what[3] == 1:
                    q, d = what[1:3]
                    dve.wait_ge(unit_done, u + 1)
                    gated_sum([(d, t) for t in range(4)], 8 + 8 * q + 4 * d, [4, 5, 6, 7] if d == 0 else [0, 1, 2, 3],
                              tmpf, GF, 8)
            normed(2)
            dve.wait_ge(s5_raw, 32)
            dve.tensor_scalar(C5[1], C5[1], -1.0, None, ALU.mult).then_inc(s5_c, 1)
            modulate(2)
            for i, (n, t) in enumerate(IN_JOBS[:8]):
                heads = (8, 4, 3)[n]
                w_ = heads * HD
                dve.wait_ge(in_squared, 8 + i + 1)
                dve.tensor_reduce(hss[:, 0:heads], sqo[:, i % 2, 0:w_].rearrange("p (h d) -> p h d", d=HD), AX,
                                  ALU.add).then_inc(in_summed, 1)
                dve.wait_ge(in_summed, 8 + i + 1)
                rsqrt_mean(hss[:, 0:heads], hss[:, 0:heads], HD)
                dst = (kn[:, t, :, 0, :] if n == 2 else
                       qn[:, t, 512 * n:512 * n + w_].rearrange("p (h d) -> p h d", d=HD))
                dve.tensor_tensor(dst, bank[4 + i % 4][:, 0:w_].rearrange("p (h d) -> p h d", d=HD),
                                  hss[:, 0:heads].unsqueeze(2).to_broadcast([P, heads, HD]),
                                  ALU.mult).then_inc(in_normed, 1)
                dve.wait_ge(in_normed, 8 + i + 1)
            for j in range(9, 18, 2):
                dve.wait_ge(qk_turned, j + 1)
                jj = j - 8
                dst = (HT[:, 512 * jj:512 * jj + 512] if jj < 6 else uT[(jj - 6) // 2][:, jj % 2, :])
                dve.tensor_copy(dst, bank[1][:, :]).then_inc(qk_dve, 1)
            dve.wait_ge(s5_turned, 2)
            dve.tensor_copy(BT[1], bank[3][:, :]).then_inc(s5_bt_dve, 1)
            dve.tensor_scalar(C5neg, C5[0], -1.0, None, ALU.mult).then_inc(s5_c, 1)

            for k in range(UNITS):
                j, d = divmod(k, 2)
                u = PAIRS * d + j
                br, bi = bank[2 * (k % 2)][:, :], bank[2 * (k % 2) + 1][:, :]
                co, si = turn[:, k % 2, 0, :], turn[:, k % 2, 1, :]
                dve.wait_ge(s5_table, k + 1)
                dve.wait_ge(s5_bu, k + 1)
                if k:
                    dve.wait_ge(s5_s, k)
                dve.tensor_tensor(z[0], br, co, ALU.mult)
                step(dve.tensor_tensor(vt[0], bi, si, ALU.mult))
                dve.tensor_tensor(z[0], z[0], vt[0], ALU.add)
                dve.tensor_tensor(z[1], bi, co, ALU.mult)
                step(dve.tensor_tensor(vt[1], br, si, ALU.mult))
                dve.sem_inc(s5_bu_used, 1)
                step(dve.tensor_tensor(z[1], z[1], vt[1], ALU.subtract))
                r = s5v[:, S_R, u:u + 1].to_broadcast([P, TOK])
                for i in range(2):
                    ins = dve.tensor_tensor_scan(z[i], r, z[i], 0.0, ALU.mult, ALU.add)
                step(ins)
                if k >= 2:
                    dve.wait_ge(s5_y, k - 1)
                co, si, zr, zi = (x[:, SEQ:TOK] for x in (co, si, z[0], z[1]))
                o = [s_out[:, k % 2, i, :] if d == 0 else s_out[:, k % 2, i, ::-1] for i in range(4)]
                dve.tensor_tensor(o[0], zr, co, ALU.mult)
                dve.tensor_tensor(o[1], zi, si, ALU.mult)
                dve.tensor_tensor(o[2], zr, si, ALU.mult)
                dve.tensor_tensor(o[3], zi, co, ALU.mult).then_inc(s5_s, 1)
            dve.wait_ge(s5_y, UNITS)
            for m in range(2):
                ins = dve.scalar_tensor_tensor(out=y5[:, m, :], in0=uT[0][:, m, CTX:], scalar=vec[:, V_D + m:V_D + m + 1],
                                               in1=bank[4 + m][:, 0:SEQ], op0=ALU.mult, op1=ALU.add)
            ins.then_inc(y5_ready, 1)
            dve.wait_ge(glu_sig, 1)
            dve.tensor_tensor(oTo[:, 6:8, :], y5s[:, :, :], y5[:, :, :], ALU.mult).then_inc(ssm_ready, 1)
            attention(ODD_JOBS, ATTN_E, oTo, 0)
            def split_unit(n, u):
                h = 2 * S_MOE + u
                dve.wait_ge(split_hi, F_UNITS + E_UNITS * n + u + 1)
                dve.tensor_tensor(part(1, h), ring[:, h % HALVES, :], part(0, h).bitcast(F32),
                                  ALU.subtract).then_inc(split_lo, 1)

            halves2 = [(half, t) for half in range(2) for t in range(2)]
            gated_sum(halves2[:1], 8 + RES_FFN, [3], tmp, G, 10)
            split_unit(0, 0)
            gated_sum(halves2[1:2], 9 + RES_FFN, [4], tmp, G, 10)
            split_unit(0, 1)
            gated_sum(halves2[2:], 10 + RES_FFN, [5, 6], tmp, G, 10)
            normed(3)
            modulate(3)

            def R(i):
                return s5v[:, i, :].rearrange("p (t e) -> p t e", t=2)

            def wide(x):
                return x.unsqueeze(2).to_broadcast([P, 2, NE])

            top = s5v[:, R_T, :]
            dve.memset(acc[:, :, :], 0.0)
            dve.memset(pick[:, :, NE, :], 0.0)
            for u in range(2, AHEAD + 1):
                split_unit(0, u)
            dve.wait_ge(logits, 1)
            step(dve.tensor_tensor(R(R_L), bank[2][:, 0:16].rearrange("p (t e) -> p t e", t=2),
                                   vec[:, V_RB:V_RB + 8].unsqueeze(1).to_broadcast([P, 2, NE]), ALU.add))
            step(dve.tensor_scalar(R(R_C), cst[:, C_IOTA:C_IOTA + 8].unsqueeze(1).to_broadcast([P, 2, NE]),
                                   -1.0, float(NE), ALU.mult, ALU.add))
            for k, (src, hot) in enumerate(((R_L, R_O1), (R_L2, R_O2))):
                step(dve.tensor_reduce(top[:, 8 + 2 * k:10 + 2 * k], R(src), AX, ALU.max))
                step(dve.tensor_tensor(R(R_EQ), R(src), wide(top[:, 8 + 2 * k:10 + 2 * k]), ALU.is_equal))
                step(dve.tensor_tensor(R(R_EQ), R(R_EQ), R(R_C), ALU.mult))
                step(dve.tensor_reduce(top[:, 12:14], R(R_EQ), AX, ALU.max))
                step(dve.tensor_tensor(R(hot), R(R_C), wide(top[:, 12:14]), ALU.is_equal))
                if k == 0:
                    step(dve.scalar_tensor_tensor(out=R(R_L2), in0=R(hot), scalar=-3.0e38, in1=R(R_L),
                                                  op0=ALU.mult, op1=ALU.add))
            step(dve.tensor_tensor(R(R_SEL), R(R_O1), R(R_O2), ALU.add))
            dve.tensor_tensor(top[:, 2:4], top[:, 10:12], top[:, 8:10], ALU.subtract).then_inc(top_gap, 1)
            dve.sem_inc(sel_ready, 1)
            dve.wait_ge(top_exp, 1)
            step(dve.tensor_scalar(top[:, 0:2], top[:, 4:6], 1.0, None, ALU.add))
            step(dve.reciprocal(top[:, 0:2], top[:, 0:2]))
            step(dve.tensor_tensor(top[:, 6:8], top[:, 0:2], top[:, 4:6], ALU.mult))
            dve.tensor_tensor(R(R_O1), R(R_O1), wide(top[:, 0:2]), ALU.mult)
            step(dve.tensor_tensor(R(R_O2), R(R_O2), wide(top[:, 6:8]), ALU.mult))
            step(dve.tensor_tensor(R(R_GATE), R(R_O1), R(R_O2), ALU.add))
            dve.wait_ge(ranks, 1)
            step(dve.tensor_copy(s5v[:, R_POS, :], bank[3][:, 0:16]))
            step(dve.tensor_scalar(s5v[:, R_POS2, :], bank[3][:, 0:16], -float(P), None, ALU.add))
            step(dve.tensor_reduce(top[:, 14:15], bank[3][:, 16:24], AX, ALU.max))
            dve.tensor_scalar(flag[:, :], top[:, 14:15], float(P), None, ALU.is_gt).then_inc(flag_ready, 1)

            def tasks(n, u, rnd):
                g = F_UNITS + E_UNITS * n
                if u < 2 * W13_SLOTS and u % 2 == 1:
                    m = u // 2
                    dve.wait_ge(e_silu, W13_SLOTS * n + m + 1)
                    dve.tensor_tensor(he[:, m % 2, :], sile[:, m % 2, :], bank[m % 2][:, 256:512],
                                      ALU.mult).then_inc(e_gated, 1)
                    if m >= 1:
                        turned(n, m - 1)
                if u == 2 * W13_SLOTS:
                    turned(n, W13_SLOTS - 1)
                if u == 2 * W13_SLOTS + GATHER_AT:
                    gathered(n + rnd + 1)
                if u == E_UNITS - 1:
                    dve.wait_ge(unit_done, g + E_UNITS)
                    dve.tensor_copy(ye[:, 512:1024], bank[5][:, :]).then_inc(y_dve, 1)

            def turned(n, m):
                dve.wait_ge(heT_hi, W13_SLOTS * n + m + 1)
                o = heTr[:, :, 2 * m:2 * m + 2, :].rearrange("p i c s -> p i (c s)")
                dve.tensor_tensor(o[:, 1], bank[2 + m % 2][:, 0:2 * P], o[:, 0].bitcast(F32),
                                  ALU.subtract).then_inc(heT_lo, 1)

            def gathered(i):
                dve.wait_ge(e_gather, 2 * i + 2)
                for c in range(4, 8):
                    ins = dve.tensor_scalar(xf[:, c, :], bank[7][:, (c - 4) * P:(c - 3) * P], coef[:, 3, c, 0:1],
                                            mod[1][:, M_SH2 + c, 0:1], ALU.mult, ALU.add)
                ins.then_inc(xf_dve, 1)
                dve.wait_ge(xe_hi, i + 1)
                dve.tensor_tensor(xer[:, 1, :, :], xf[:, :, :], xer[:, 0, :, :].bitcast(F32),
                                  ALU.subtract).then_inc(xe_lo, 1)

            def scattered(n):
                for k in range(4):
                    h, t = divmod(k, 2)
                    dve.wait_ge(e_scatter, 4 * n + k + 1)
                    x = acc[:, t, h * 512:(h + 1) * 512]
                    dve.tensor_tensor(x, x, bank[6 + k % 2][:, :], ALU.add).then_inc(e_added, 1)

            def expert(n, rnd, last):
                for u in range(1, E_UNITS):
                    if u + AHEAD < E_UNITS:
                        split_unit(n, u + AHEAD)
                    elif not last:
                        split_unit(n + 1, u + AHEAD - E_UNITS)
                    tasks(n, u, rnd)
                if not last:
                    split_unit(n + 1, AHEAD)
                scattered(n)

            def experts(rnd):
                iota, rank = cst[:, C_IOTA:C_IOTA + P], (R_POS, R_POS2)[rnd]
                for table, times in ((pick, R_SEL), (gpick, R_GATE)):
                    for e in range(NE):
                        for t in range(2):
                            c = 8 * t + e
                            ins = dve.tensor_scalar(table[:, t, e, :], iota, s5v[:, rank, c:c + 1],
                                                    s5v[:, times, c:c + 1], ALU.is_equal, ALU.mult)
                    ins.then_inc(pick_ready, 1)
                for g in range(1, 4, 2):
                    dve.wait_ge(gpick_turned, 4 * rnd + g + 1)
                    dve.tensor_copy(gTall[:, 2 * g:2 * g + 2, :].rearrange("p e t -> p (e t)"),
                                    bank[2 + g][:, :]).then_inc(gta_dve, 1)
                gathered((NE + 1) * rnd)
                for u in range(AHEAD + 1) if rnd else ():
                    split_unit(NE * rnd, u)
                with dve.Fori(0, NE - 1) as e:
                    expert(e + NE * rnd, rnd, False)
                expert(NE - 1 + NE * rnd, rnd, True)

            dve.sem_inc(e_gated, 2)
            dve.sem_inc(heT_lo, 2)
            dve.sem_inc(e_added, 1)
            experts(0)
            crowded = dve.value_load(flag[0:1, 0:1], min_val=0, max_val=1)
            with dve.If(crowded > 0):
                experts(1)
            for t in range(2):
                for h in range(2):
                    x = acc[:, t, h * 512:(h + 1) * 512]
                    step(dve.tensor_tensor(x, x, G2[:, h * 512:(h + 1) * 512], ALU.mult))
                    o = X[:, t, h * 512:(h + 1) * 512]
                    dve.tensor_tensor(o, o, x, ALU.add).then_inc(final_ready, 1)

        @block.gpsimd
        def _(pool):
            steps = [0]

            def step(ins):
                steps[0] += 1
                ins.then_inc(pool_step, 1)
                pool.wait_ge(pool_step, steps[0])

            def residual(half_tiles, r0, buf):
                for k, (half, t) in enumerate(half_tiles):
                    r = r0 + k
                    pool.wait_ge(res_gated, r + 1)
                    x = X[:, t, half * 512:(half + 1) * 512]
                    pool.tensor_tensor(x, x, buf[:, r % 2, :], ALU.add).then_inc(res_done, 1)

            def cmul(o, x, y, t):
                pool.tensor_tensor(t[0], x[0], y[0], ALU.mult)
                pool.tensor_tensor(t[1], x[1], y[1], ALU.mult)
                pool.tensor_tensor(t[2], x[0], y[1], ALU.mult)
                step(pool.tensor_tensor(t[3], x[1], y[0], ALU.mult))
                pool.tensor_tensor(o[0], t[0], t[1], ALU.subtract)
                step(pool.tensor_tensor(o[1], t[2], t[3], ALU.add))

            def V(i, n=1):
                return s5v[:, i:i + n, :].rearrange("p a u -> p (a u)")

            pool.wait_ge(vec_landed, 16)
            pool.wait_ge(s5_rden, 1)
            step(pool.tensor_scalar(V(3), vec[:, V_STEP:V_STEP + 16], -120.0, 88.0, ALU.max, ALU.min))
            step(pool.tensor_scalar(V(4), V(3), float(1 / np.log(2)), ROUND, ALU.mult, ALU.add))
            step(pool.tensor_scalar(V(4), V(4), -ROUND, None, ALU.add))
            for part in LN2_PARTS:
                step(pool.tensor_scalar(V(5), V(4), -part, None, ALU.mult))
                step(pool.tensor_tensor(V(3), V(3), V(5), ALU.add))
            step(pool.memset(V(0), 1.0))
            for n in range(9, 0, -1):
                step(pool.tensor_tensor(V(0), V(0), V(3), ALU.mult))
                step(pool.tensor_scalar(V(0), V(0), 1.0 / n, 1.0, ALU.mult, ALU.add))
            step(pool.tensor_scalar(V(4), V(4), 127.0, 0.0, ALU.add, ALU.max))
            step(pool.tensor_scalar(V(5).bitcast(I32), V(4), float(1 << 23), None, ALU.mult))
            step(pool.tensor_tensor(V(0), V(0), V(5), ALU.mult))
            W_, E_, T_, K_ = (V(3, 2), V(5, 2)), (V(7, 2), V(9, 2)), [V(11 + 2 * i, 2) for i in range(4)], V(19)
            pool.memset(V(3, 4), 0.0)
            step(pool.memset(V(7, 4), 0.0))
            step(pool.tensor_tensor(V(3), vec[:, V_ARE:V_ARE + 16], V(0), ALU.mult))
            step(pool.tensor_scalar(V(3), V(3), -87.0, 87.0, ALU.max, ALU.min))
            step(pool.tensor_tensor(V(6), vec[:, V_AIM:V_AIM + 16], V(0), ALU.mult))
            step(pool.tensor_scalar(K_, V(6), 1.0 / (2 * np.pi), ROUND, ALU.mult, ALU.add))
            step(pool.tensor_scalar(K_, K_, -ROUND, None, ALU.add))
            for part in TURN_PARTS:
                step(pool.tensor_scalar(V(20), K_, -part, None, ALU.mult))
                step(pool.tensor_tensor(V(6), V(6), V(20), ALU.add))
            step(pool.tensor_scalar(V(3, 4), V(3, 4), 1.0 / 256, None, ALU.mult))
            step(pool.tensor_scalar(E_[0], E_[0], 1.0, None, ALU.add))
            for n in range(8, 1, -1):
                cmul(E_, E_, W_, T_)
                step(pool.tensor_scalar(V(7, 4), V(7, 4), 1.0 / n, None, ALU.mult))
                step(pool.tensor_scalar(E_[0], E_[0], 1.0, None, ALU.add))
            cmul(E_, E_, W_, T_)
            for _ in range(8):
                step(pool.tensor_scalar(W_[0], E_[0], 2.0, None, ALU.add))
                cmul(E_, E_, (W_[0], E_[1]), T_)
            step(pool.tensor_tensor(V(3), V(7), V(8), ALU.mult))
            step(pool.tensor_tensor(V(3), V(3), V(7), ALU.add))
            step(pool.tensor_tensor(V(3), V(3), V(8), ALU.add))
            step(pool.tensor_tensor(V(4), V(7), V(10), ALU.mult))
            step(pool.tensor_tensor(V(4), V(4), V(10), ALU.add))
            are, aim = vec[:, V_ARE:V_ARE + 16], vec[:, V_AIM:V_AIM + 16]
            step(pool.tensor_scalar(V(11), aim, -1.0, None, ALU.mult))
            cmul((V(5), V(6)), (V(3), V(4)), (are, V(11)), [V(12), V(13), V(14), V(15)])
            step(pool.tensor_tensor(V(5), V(5), V(1), ALU.mult))
            step(pool.tensor_tensor(V(6), V(6), V(1), ALU.mult))
            step(pool.tensor_scalar(V(S_R), V(7), 1.0, None, ALU.add))
            step(pool.tensor_scalar(V(S_PW), V(8), 1.0, None, ALU.add))
            step(pool.tensor_scalar(V(S_PW + 1), V(10), 0.0, None, ALU.add))
            for j in range(8):
                n, t = divmod(j, 4)
                pool.wait_ge(in_normed, j + 1)
                hg = H_EQ if n == 0 else H_EK
                v = hn[:, 1 + n, t, :].rearrange("p (h d) -> p h d", d=HD)
                pool.tensor_tensor(v, v, vec[:, V_HEAD + hg * HD:V_HEAD + (hg + 1) * HD].unsqueeze(1)
                                   .to_broadcast([P, 8, HD]), ALU.mult).then_inc(head_ready, 1)

            def load_bias(h):
                for t in range(2):
                    for q in range(2):
                        row = 2 * t + q
                        src = bass.AP(a["rpb"].tensor, (h * NA_DR + 7 - row) * RPB_PAD,
                                      [[1, GRID_W], [RPB_PAD, ROWS], [1, GRID_W]])
                        pool.dma_start(bias_raw[64 * q:64 * q + 64, h % 2, t * SEQ:(t + 1) * SEQ]
                                       .rearrange("p (r c) -> p r c", r=ROWS), src).then_inc(bias_landed[h % 2], 16)

            load_bias(0)
            for h in range(NA_HEADS):
                if h + 1 < NA_HEADS:
                    if h >= 1:
                        pool.wait_ge(bias_ready, h)
                    load_bias(h + 1)
                pool.wait_ge(bias_landed[h % 2], 64 * (h // 2 + 1))
                if h >= 2:
                    pool.wait_ge(bias_used, 2 * (h - 1))
                b = bias[:, h % 2, :].rearrange("p (r c) -> p r c", c=GRID_W)
                raw = bias_raw[:, h % 2, :].rearrange("p (r c) -> p r c", c=GRID_W)
                pool.tensor_tensor(b, raw[:, :, ::-1], cst[:, C_MASK:C_MASK + GRID_W].unsqueeze(1)
                                   .to_broadcast([P, 2 * ROWS, GRID_W]), ALU.add).then_inc(bias_ready, 1)
            halves4 = [(half, t) for half in range(2) for t in range(4)]
            residual(halves4, 0, tmp)
            for q in range(len(FG)):
                residual(halves4, 8 + 8 * q, tmpf)

            pool.wait_ge(s5_raw, 32)
            cf = [V(5 + i).unsqueeze(2).to_broadcast([P, UNITS, 32]) for i in range(2)]
            for i, (x, y, op) in enumerate(((0, 1, ALU.subtract), (1, 0, ALU.add))):
                pool.tensor_tensor(b_bar[i], b_raw[x], cf[0], ALU.mult)
                step(pool.tensor_tensor(b_tmp, b_raw[y], cf[1], ALU.mult))
                ins = pool.tensor_tensor(b_bar[i], b_bar[i], b_tmp, op)
                if i == 0:
                    step(ins)
            ins.then_inc(s5_bbar, 1)


            def powers(tab, m, n, row):
                pw = [V(row + i).unsqueeze(2).to_broadcast([P, UNITS, m]) for i in range(2)]
                t = [x[:, 0:UNITS * m].rearrange("p (u n) -> p u n", u=UNITS) for x in p4]
                cmul([x[:, :, m:2 * m] for x in tab], [x[:, :, 0:m] for x in tab], pw, t)

            for tab in (lo, hi):
                for i in range(2):
                    step(pool.memset(tab[i][:, :, 0:1], 1.0 - i))
            for k in range(9):
                row = S_PW
                tab, m = (lo, 1 << k) if k < 4 else (hi, 1 << (k - 4))
                powers(tab, m, 2 * m, row)
                if k < 8:
                    cmul((V(S_PW), V(S_PW + 1)), (V(S_PW), V(S_PW + 1)), (V(S_PW), V(S_PW + 1)),
                         [V(11), V(12), V(13), V(14)])
            for i, (n, t) in enumerate(IN_JOBS[:8]):
                heads = (8, 4, 3)[n]
                pool.wait_ge(in_normed, 8 + i + 1)
                v = (kn[:, t, :, 0, :] if n == 2 else
                     qn[:, t, 512 * n:512 * n + heads * HD].rearrange("p (h d) -> p h d", d=HD))
                hg = H_OK if n == 2 else H_OQ

                def over_heads(x, w=HD):
                    return x.unsqueeze(1).to_broadcast([P, heads, w])

                ins = pool.tensor_tensor(v, v, over_heads(vec[:, V_HEAD + hg * HD:V_HEAD + (hg + 1) * HD]), ALU.mult)
                if t < LAT_TILES:
                    step(ins)
                    cos = cst[:, C_COS + t * HD:C_COS + (t + 1) * HD]
                    sin = cst[:, C_SIN + t * HD:C_SIN + (t + 1) * HD]
                    r = rope_t[:, 0:heads * HD].rearrange("p (h d) -> p h d", d=HD)
                    pool.tensor_tensor(r[:, :, 0::2], v[:, :, 1::2], over_heads(sin[:, 0::2], HD // 2), ALU.mult)
                    step(pool.tensor_tensor(r[:, :, 1::2], v[:, :, 0::2], over_heads(sin[:, 1::2], HD // 2), ALU.mult))
                    step(pool.tensor_tensor(v, v, over_heads(cos), ALU.mult))
                    ins = pool.tensor_tensor(v, v, r, ALU.add)
                if n == 2:
                    step(ins)
                    ins = pool.tensor_copy(kn[:, t, :, 1, :], kn[:, t, :, 0, :])
                ins.then_inc(head_ready, 1)

            for k in range(UNITS):
                j, d = divmod(k, 2)
                u = PAIRS * d + j
                h = [x[:, u, :].unsqueeze(2).to_broadcast([P, 32, 16]) for x in hi]
                l = [x[:, u, :].unsqueeze(1).to_broadcast([P, 32, 16]) for x in lo]
                o = [turn[:, k % 2, i, :].rearrange("p (a b) -> p a b", a=32) for i in range(2)]
                t = [x.rearrange("p (a b) -> p a b", a=32) for x in pt]
                if k >= 2:
                    pool.wait_ge(s5_s, k - 1)
                pool.tensor_tensor(t[0], h[0], l[0], ALU.mult)
                step(pool.tensor_tensor(t[1], h[1], l[1], ALU.mult))
                step(pool.tensor_tensor(o[0], t[0], t[1], ALU.subtract))
                pool.tensor_tensor(t[0], h[0], l[1], ALU.mult)
                step(pool.tensor_tensor(t[1], h[1], l[0], ALU.mult))
                pool.tensor_tensor(o[1], t[0], t[1], ALU.add).then_inc(s5_table, 1)
                pool.wait_ge(s5_table, k + 1)
            residual([(half, t) for half in range(2) for t in range(2)], 8 + RES_FFN, tmp)

            def experts(rnd):
                pool.wait_ge(gta_act, 2 * (rnd + 1))
                pool.wait_ge(gta_dve, 2 * (rnd + 1))
                with pool.Fori(0, NE) as e:
                    n = e + NE * rnd
                    pool.wait_ge(e_gather, 2 * (n + rnd) + 4)
                    pool.tensor_copy(gTe[:, :], gTall[:, bass.ds(e, 1), :]
                                     .rearrange("p o t -> p (o t)")).then_inc(gte_ready, 1)

            experts(0)
            pool.wait_ge(flag_ready, 1)
            crowded = pool.value_load(flag[0:1, 0:1], min_val=0, max_val=1)
            with pool.If(crowded > 0):
                experts(1)


_OUTS = [((1, SEQ, D), "float32")]


def host_layout(inp):
    f = {k: np.ascontiguousarray(np.asarray(v)) for k, v in inp.items()}
    v = np.zeros((P, V_ALL), np.float32)

    def cols(x):
        return x.reshape(-1, P).T

    v[:, V_COND:V_COND + 16] = np.stack([cols(f["c"][0]), cols(f["c_ctx"])], 2).reshape(P, 16)
    for q, n in enumerate(("ev_norm_mix", "ev_norm_ffn", "od_norm_mix", "od_norm_ffn")):
        v[:, V_NORM + 8 * q:V_NORM + 8 * q + 8] = cols(f[n][0])
    for q, n in enumerate(("ev_mod_b", "od_mod_b")):
        v[:, V_MODB + 48 * q:V_MODB + 48 * q + 48] = cols(f[n][0])

    def states(x):
        return x.reshape(2, PAIRS, 2 * S5_STATE).transpose(2, 0, 1).reshape(P, UNITS)

    v[:, V_ARE:V_ARE + 16] = states(f["od_s5_a_re"][0])
    v[:, V_AIM:V_AIM + 16] = states(f["od_s5_a_im"][0])
    v[:, V_STEP:V_STEP + 16] = states(np.repeat(f["od_s5_log_step"][0][:, :, None], S5_STATE, 2))
    v[:, V_D:V_D + 2] = cols(f["od_s5_d"][0])
    v[:, V_GLUB:V_GLUB + 2] = cols(f["od_s5_glu_b"][0])
    for q, n in enumerate(("ev_q_gain", "ev_k_gain", "od_q_gain", "od_k_gain")):
        v[:, V_HEAD + HD * q:V_HEAD + HD * (q + 1)] = f[n][0][None, :]
    v[:, V_RW:V_RW + 64] = f["od_router_w"][0].reshape(DC, P, NE).transpose(1, 0, 2).reshape(P, 64)
    v[:, V_RB:V_RB + 8] = f["od_router_b"][0][None, :]
    rpb = np.zeros((NA_HEADS, NA_DR, RPB_PAD), np.float32)
    rpb[:, :, 63 - (NA_KW - 1):63 + NA_KW] = f["ev_rpb"][0][:, :, ::-1]
    bb = np.zeros((2, 2, S5_STATE, UNITS, 2, S5_DIM), np.float32)
    cc = np.zeros((2, 2, S5_STATE, UNITS, 2, S5_DIM), np.float32)
    for part, s in enumerate(("re", "im")):
        for g in range(2):
            bb[part, g, :, :, g, :] = (f[f"od_s5_b_{s}"][0].reshape(2, PAIRS, 2, S5_STATE, S5_DIM)[:, :, g]
                                       .transpose(2, 0, 1, 3).reshape(S5_STATE, UNITS, S5_DIM))
            cc[part, g, :, :, g, :] = (f[f"od_s5_c_{s}"][0].reshape(2, PAIRS, 2, S5_DIM, S5_STATE)[:, :, g]
                                       .transpose(3, 0, 1, 2).reshape(S5_STATE, UNITS, S5_DIM))
    arrays = {"vec": v, "cst": constants(), "dft": dft_constants(), "rpb": rpb,
              "s5b": bb.reshape(2, P, UNITS * 32), "s5c": cc.reshape(2, P, UNITS * 32)}
    for n in ("x", "ctx", "ev_mod_w", "ev_w_in", "ev_w_out", "ev_ffn_w1", "ev_ffn_w3", "ev_ffn_w2", "od_mod_w",
              "od_w_in", "od_s5_glu_w", "od_w_out", "od_router_w", "od_exp_w1", "od_exp_w3", "od_exp_w2"):
        arrays[n] = f[n]
    return arrays


def kernel(**inputs):
    import concourse.bacc as bacc
    from concourse.bass_utils import run_bass_kernel_spmd

    nc = bacc.Bacc("TRN2", target_bir_lowering=False, num_devices=1)
    arrays = host_layout(inputs)
    a = {n: nc.dram_tensor(f"in_{n}", x.shape, mybir.dt.from_np(x.dtype), kind="ExternalInput").ap()
         for n, x in arrays.items()}
    out = nc.dram_tensor("out_0", _OUTS[0][0], F32, kind="ExternalOutput").ap()
    build(nc, a, out)
    r = run_bass_kernel_spmd(nc, [{f"in_{n}": x for n, x in arrays.items()}], core_ids=[0])
    return r.results[0]["out_0"]
```
